# Optimizing a Trainium2 kernel written in Bass

```python
import math, functools
import jax, jax.numpy as jnp
from jax import lax
import numpy as np

D_MODEL = 1024
BATCH = 1
SEQ = 512
DEPTH = 1
DEC_BATCH = 8
DEC_SEQ = 4
PAST_LEN = 256
PAGE_SIZE = 128

RET_HEADS = 4
RET_DK = 128
RET_DV = 128
RET_WIDTH = RET_HEADS * RET_DV
RET_CHUNK = 128
MOBA_HEADS = 8
MOBA_DH = 64
MOBA_WIDTH = MOBA_HEADS * MOBA_DH
MOBA_BLOCK = 256
MOBA_TOPK = 3
MOBA_QBLOCK = 128
N_GROUPS = 4
EXPERTS_PER_GROUP = 8
N_EXPERTS = N_GROUPS * EXPERTS_PER_GROUP
EXPERT_TOPK = 2
EXPERT_HIDDEN = 128
ALPHA = (2 * DEPTH) ** 0.25
BETA = (8 * DEPTH) ** -0.25
LN_EPS = 1e-5
W_IN = 4 * RET_WIDTH + 3 * MOBA_WIDTH + 2 * D_MODEL

kernel_name = "hybrid_retention_moba_hmoe_step"

F32 = jnp.float32

def retention_gammas():
    return jnp.asarray(1.0 - 2.0 ** (-5.0 - np.arange(RET_HEADS)), dtype=F32)

def alibi_slopes():
    return jnp.asarray(2.0 ** (-8.0 * np.arange(1, MOBA_HEADS + 1) / MOBA_HEADS), dtype=F32)

def layer_norm(x, g, b):
    xf = x.astype(F32)
    mu = jnp.mean(xf, axis=-1, keepdims=True)
    var = jnp.mean(jnp.square(xf - mu), axis=-1, keepdims=True)
    return ((xf - mu) * lax.rsqrt(var + LN_EPS) * g + b).astype(x.dtype)

def retention_chunk(state, q, k, v):
    L = q.shape[2]
    log_g = jnp.log(retention_gammas())
    idx = jnp.arange(L, dtype=F32)
    diff = idx[:, None] - idx[None, :]
    decay = jnp.where(diff >= 0, jnp.exp(log_g[:, None, None] * jnp.maximum(diff, 0.0)), 0.0)
    scores = jnp.einsum('bhid,bhjd->bhij', q, k) * decay
    inner = jnp.einsum('bhij,bhjv->bhiv', scores, v)
    q_dec = q * jnp.exp(log_g[:, None] * (idx + 1.0))[:, :, None]
    cross = jnp.einsum('bhid,bhdv->bhiv', q_dec, state)
    k_dec = k * jnp.exp(log_g[:, None] * (L - 1.0 - idx))[:, :, None]
    new_state = state * jnp.exp(log_g * L)[:, None, None] + jnp.einsum('bhjd,bhjv->bhdv', k_dec, v)
    return new_state, inner + cross

def retention_prompt(q, k, v):
    B, H, S, dk = q.shape
    n_c = S // RET_CHUNK
    to_chunks = lambda t: t.reshape(B, H, n_c, RET_CHUNK, t.shape[-1]).transpose(2, 0, 1, 3, 4)
    s0 = jnp.zeros((B, H, dk, v.shape[-1]), F32)
    s_fin, o = lax.scan(lambda s, c: retention_chunk(s, *c), s0, (to_chunks(q), to_chunks(k), to_chunks(v)))
    o = o.transpose(1, 2, 0, 3, 4).reshape(B, H, S, v.shape[-1])
    return o, s_fin

def retention_sample(state, q, k, v):
    s_new, o = retention_chunk(state.astype(F32), q, k, v)
    return o, s_new

def moba_blocks(k, v):
    B, H, T, dh = k.shape
    nb = -(-T // MOBA_BLOCK)
    pad = ((0, 0), (0, 0), (0, nb * MOBA_BLOCK - T), (0, 0))
    k_blk = jnp.pad(k, pad).reshape(B, H, nb, MOBA_BLOCK, dh)
    v_blk = jnp.pad(v, pad).reshape(B, H, nb, MOBA_BLOCK, dh)
    k_mean = jnp.mean(k_blk.astype(F32), axis=3).astype(k.dtype)
    return k_blk, v_blk, k_mean

def moba_query_block(q, q_pos0, k_blk, v_blk, k_mean):
    B, H, Q, dh = q.shape
    nb = k_blk.shape[2]
    scale = dh ** -0.5
    slopes = alibi_slopes()[None, :, None, None]
    own = q_pos0 // MOBA_BLOCK
    q_pos = q_pos0 + jnp.arange(Q)
    gate = jnp.einsum('bhqd,bhnd->bhqn', q, k_mean).astype(F32)
    gate = jnp.where(jnp.arange(nb) < own, gate, -jnp.inf)
    n_sel = min(MOBA_TOPK, nb)
    gval, sel = lax.top_k(gate, n_sel)
    sel_ok = jnp.isfinite(gval)
    bi = jnp.arange(B)[:, None, None, None]
    hi = jnp.arange(H)[None, :, None, None]
    kg = k_blk[bi, hi, sel]
    vg = v_blk[bi, hi, sel]
    key_pos = sel[..., None] * MOBA_BLOCK + jnp.arange(MOBA_BLOCK)
    dist = (q_pos[None, None, :, None, None] - key_pos).astype(F32)
    l_sel = jnp.einsum('bhqd,bhqnkd->bhqnk', q, kg).astype(F32) * scale - slopes[..., None] * dist
    l_sel = jnp.where(sel_ok[..., None], l_sel, -jnp.inf).reshape(B, H, Q, n_sel * MOBA_BLOCK)
    k_own = lax.dynamic_index_in_dim(k_blk, own, axis=2, keepdims=False)
    v_own = lax.dynamic_index_in_dim(v_blk, own, axis=2, keepdims=False)
    own_pos = own * MOBA_BLOCK + jnp.arange(MOBA_BLOCK)
    dist_own = (q_pos[:, None] - own_pos[None, :]).astype(F32)
    l_own = jnp.einsum('bhqd,bhkd->bhqk', q, k_own).astype(F32) * scale - slopes * dist_own
    l_own = jnp.where(dist_own >= 0, l_own, -jnp.inf)
    p = jax.nn.softmax(jnp.concatenate([l_sel, l_own], axis=-1), axis=-1).astype(v_blk.dtype)
    p_sel = p[..., :n_sel * MOBA_BLOCK].reshape(B, H, Q, n_sel, MOBA_BLOCK)
    p_own = p[..., n_sel * MOBA_BLOCK:]
    return (jnp.einsum('bhqnk,bhqnkd->bhqd', p_sel, vg)
            + jnp.einsum('bhqk,bhkd->bhqd', p_own, v_own))

def moba_prompt(q, k, v):
    B, H, S, dh = q.shape
    k_blk, v_blk, k_mean = moba_blocks(k, v)
    n_q = S // MOBA_QBLOCK
    qc = q.reshape(B, H, n_q, MOBA_QBLOCK, dh).transpose(2, 0, 1, 3, 4)
    o = lax.map(lambda a: moba_query_block(a[1], a[0] * MOBA_QBLOCK, k_blk, v_blk, k_mean),
                (jnp.arange(n_q), qc))
    return o.transpose(1, 2, 0, 3, 4).reshape(B, H, S, dh)

def moba_sample(q, k, v, past_k, past_v):
    past = past_k.shape[1]
    k_all = jnp.concatenate([past_k.transpose(0, 2, 1, 3), k], axis=2)
    v_all = jnp.concatenate([past_v.transpose(0, 2, 1, 3), v], axis=2)
    k_blk, v_blk, k_mean = moba_blocks(k_all, v_all)
    return moba_query_block(q, past, k_blk, v_blk, k_mean)

def token_mixer(x, ret_fn, moba_fn, w_in, b_merge, gn_g, w_br_ret, w_br_moba, w_out):
    B, L, _ = x.shape
    h = jnp.einsum('bld,de->ble', x, w_in)
    cuts = [RET_WIDTH, 2 * RET_WIDTH, 3 * RET_WIDTH, 4 * RET_WIDTH,
            4 * RET_WIDTH + MOBA_WIDTH, 4 * RET_WIDTH + 2 * MOBA_WIDTH,
            4 * RET_WIDTH + 3 * MOBA_WIDTH, 4 * RET_WIDTH + 3 * MOBA_WIDTH + D_MODEL]
    rq, rk, rv, rg, mq, mk, mv, ga, gb = jnp.split(h, cuts, axis=-1)
    heads = lambda t, n, d: t.reshape(B, L, n, d).transpose(0, 2, 1, 3)
    o_r, ret_state = ret_fn(heads(rq, RET_HEADS, RET_DK).astype(F32),
                            heads(rk, RET_HEADS, RET_DK).astype(F32) * RET_DK ** -0.5,
                            heads(rv, RET_HEADS, RET_DV).astype(F32))
    mu = jnp.mean(o_r, axis=-1, keepdims=True)
    var = jnp.mean(jnp.square(o_r - mu), axis=-1, keepdims=True)
    o_r = ((o_r - mu) * lax.rsqrt(var + LN_EPS)).transpose(0, 2, 1, 3).reshape(B, L, RET_WIDTH) * gn_g
    o_r = (jax.nn.silu(rg.astype(F32)) * o_r).astype(x.dtype)
    mk_h = mk.reshape(B, L, MOBA_HEADS, MOBA_DH)
    mv_h = mv.reshape(B, L, MOBA_HEADS, MOBA_DH)
    o_m = moba_fn(heads(mq, MOBA_HEADS, MOBA_DH), mk_h.transpose(0, 2, 1, 3), mv_h.transpose(0, 2, 1, 3))
    o_m = o_m.transpose(0, 2, 1, 3).reshape(B, L, MOBA_WIDTH)
    gates = jax.nn.sigmoid(jnp.concatenate([ga, gb], axis=-1).astype(F32) + b_merge)
    merged = (gates[..., :D_MODEL] * jnp.einsum('blr,rd->bld', o_r, w_br_ret).astype(F32)
              + gates[..., D_MODEL:] * jnp.einsum('blm,md->bld', o_m, w_br_moba).astype(F32))
    y = jnp.einsum('bld,de->ble', merged.astype(x.dtype), w_out)
    return y, (mk_h, mv_h, ret_state)

def hier_moe(x, w_rg, b_rg, w_re, b_re, w_eg, w_eu, w_ed):
    B, L, D = x.shape
    t = x.reshape(B * L, D)
    g_logit = jnp.einsum('td,dg->tg', t, w_rg).astype(F32) + b_rg
    g_idx = jnp.argmax(g_logit, axis=-1)
    g_w = jnp.take_along_axis(jax.nn.softmax(g_logit, axis=-1), g_idx[:, None], axis=-1)[:, 0]
    e_logit = jnp.einsum('td,gde->tge', t, w_re).astype(F32) + b_re
    e_logit = jnp.take_along_axis(e_logit, g_idx[:, None, None], axis=1)[:, 0]
    e_val, e_idx = lax.top_k(e_logit, EXPERT_TOPK)
    e_w = jax.nn.softmax(e_val, axis=-1) * g_w[:, None]
    gid = g_idx[:, None] * EXPERTS_PER_GROUP + e_idx
    combine = jnp.sum(jax.nn.one_hot(gid, N_EXPERTS, dtype=F32) * e_w[..., None], axis=1)
    hid = (jax.nn.silu(jnp.einsum('td,edf->tef', t, w_eg).astype(F32))
           * jnp.einsum('td,edf->tef', t, w_eu).astype(F32))
    out = jnp.einsum('tef,efd->td', (hid * combine[:, :, None]).astype(x.dtype), w_ed)
    return out.reshape(B, L, D)

def decoder_layer(x, ret_fn, moba_fn, w_in, b_merge, gn_g, w_br_ret, w_br_moba, w_out, ln1_g, ln1_b,
                  w_rg, b_rg, w_re, b_re, w_eg, w_eu, w_ed, ln2_g, ln2_b):
    y, st = token_mixer(x, ret_fn, moba_fn, w_in, b_merge, gn_g, w_br_ret, w_br_moba, w_out)
    x = layer_norm(ALPHA * x + y, ln1_g, ln1_b)
    x = layer_norm(ALPHA * x + hier_moe(x, w_rg, b_rg, w_re, b_re, w_eg, w_eu, w_ed), ln2_g, ln2_b)
    return x, st

def setup_inputs(seed: int = 0) -> dict:
    key = jax.random.key(seed)
    ks = jax.random.split(key, 32)
    n = lambda i, shape, s: jax.random.normal(ks[i], shape, F32) * s
    n_pages = PAST_LEN // PAGE_SIZE
    used = DEC_BATCH * n_pages
    n_pool = used + max(1, used // 4)
    page_table = jax.random.permutation(ks[0], n_pool)[:used].reshape(DEC_BATCH, n_pages).astype(jnp.int32)
    col_scale = jnp.concatenate([
        jnp.ones((2 * RET_WIDTH,), F32), jnp.full((RET_WIDTH,), BETA, F32), jnp.ones((RET_WIDTH,), F32),
        jnp.ones((2 * MOBA_WIDTH,), F32), jnp.full((MOBA_WIDTH,), BETA, F32), jnp.ones((2 * D_MODEL,), F32)])
    return {
        "x_prompt": n(1, (BATCH, SEQ, D_MODEL), 1.0),
        "x_sample": n(2, (DEC_BATCH, DEC_SEQ, D_MODEL), 1.0),
        "cache_k": n(3, (DEPTH, n_pool, PAGE_SIZE, MOBA_HEADS, MOBA_DH), 1.0),
        "cache_v": n(4, (DEPTH, n_pool, PAGE_SIZE, MOBA_HEADS, MOBA_DH), 1.0),
        "state_ret": n(5, (DEPTH, DEC_BATCH, RET_HEADS, RET_DK, RET_DV), 1.0),
        "page_table": page_table,
        "w_in": n(6, (DEPTH, D_MODEL, W_IN), D_MODEL ** -0.5) * col_scale,
        "b_merge": n(7, (DEPTH, 2 * D_MODEL), 0.01),
        "gn_g": 1.0 + n(8, (DEPTH, RET_WIDTH), 0.01),
        "w_br_ret": n(9, (DEPTH, RET_WIDTH, D_MODEL), BETA * RET_WIDTH ** -0.5),
        "w_br_moba": n(10, (DEPTH, MOBA_WIDTH, D_MODEL), BETA * MOBA_WIDTH ** -0.5),
        "w_out": n(11, (DEPTH, D_MODEL, D_MODEL), BETA * D_MODEL ** -0.5),
        "ln1_g": 1.0 + n(12, (DEPTH, D_MODEL), 0.01),
        "ln1_b": n(13, (DEPTH, D_MODEL), 0.01),
        "w_router_group": n(14, (DEPTH, D_MODEL, N_GROUPS), D_MODEL ** -0.5),
        "b_router_group": n(15, (DEPTH, N_GROUPS), 0.01),
        "w_router_expert": n(16, (DEPTH, N_GROUPS, D_MODEL, EXPERTS_PER_GROUP), D_MODEL ** -0.5),
        "b_router_expert": n(17, (DEPTH, N_GROUPS, EXPERTS_PER_GROUP), 0.01),
        "w_exp_gate": n(18, (DEPTH, N_EXPERTS, D_MODEL, EXPERT_HIDDEN), D_MODEL ** -0.5),
        "w_exp_up": n(19, (DEPTH, N_EXPERTS, D_MODEL, EXPERT_HIDDEN), BETA * D_MODEL ** -0.5),
        "w_exp_down": n(20, (DEPTH, N_EXPERTS, EXPERT_HIDDEN, D_MODEL), BETA * EXPERT_HIDDEN ** -0.5),
        "ln2_g": 1.0 + n(21, (DEPTH, D_MODEL), 0.01),
        "ln2_b": n(22, (DEPTH, D_MODEL), 0.01),
    }

def reference(x_prompt, x_sample, cache_k, cache_v, state_ret, page_table, w_in, b_merge, gn_g,
              w_br_ret, w_br_moba, w_out, ln1_g, ln1_b, w_router_group, b_router_group,
              w_router_expert, b_router_expert, w_exp_gate, w_exp_up, w_exp_down, ln2_g, ln2_b):
    db, n_pages = page_table.shape
    yp, ys = x_prompt, x_sample
    kp, vp, sp, ksm, vsm, ssm = [], [], [], [], [], []
    for l in range(DEPTH):
        lw = (w_in[l], b_merge[l], gn_g[l], w_br_ret[l], w_br_moba[l], w_out[l], ln1_g[l], ln1_b[l],
              w_router_group[l], b_router_group[l], w_router_expert[l], b_router_expert[l],
              w_exp_gate[l], w_exp_up[l], w_exp_down[l], ln2_g[l], ln2_b[l])
        yp, (k_p, v_p, s_p) = decoder_layer(yp, retention_prompt, moba_prompt, *lw)
        past_k = cache_k[l][page_table].reshape(db, n_pages * PAGE_SIZE, MOBA_HEADS, MOBA_DH)
        past_v = cache_v[l][page_table].reshape(db, n_pages * PAGE_SIZE, MOBA_HEADS, MOBA_DH)
        ys, (k_s, v_s, s_s) = decoder_layer(
            ys, functools.partial(retention_sample, state_ret[l]),
            functools.partial(moba_sample, past_k=past_k, past_v=past_v), *lw)
        kp.append(k_p); vp.append(v_p); sp.append(s_p)
        ksm.append(k_s); vsm.append(v_s); ssm.append(s_s)
    return (yp, ys, jnp.stack(kp), jnp.stack(vp), jnp.stack(sp),
            jnp.stack(ksm), jnp.stack(vsm), jnp.stack(ssm))


_drawn_inputs = setup_inputs


def setup_inputs(seed=0):
    import zlib

    import numpy as np

    out = dict(_drawn_inputs(seed))
    spreads = {}
    factors = {'b_merge': 8.0,
     'gn_g': 8.0,
     'ln1_g': 4.636,
     'ln1_b': 4.558,
     'b_router_group': 24.851,
     'b_router_expert': 8.0,
     'ln2_g': 29.745,
     'ln2_b': 30.82}
    for name, (base, spread) in spreads.items():
        noise = np.random.default_rng([zlib.crc32(name.encode()), seed]).standard_normal(out[name].shape)
        drawn = base * np.exp(spread * noise) if base else spread * noise
        out[name] = __import__('jax').numpy.asarray(drawn.astype(out[name].dtype))
    for name, factor in factors.items():
        out[name] = (out[name] * factor).astype(out[name].dtype)
    return out
```

```python
from contextlib import ExitStack

import numpy as np

import concourse.bass as bass
from concourse import mybir

F32 = mybir.dt.float32
I32 = mybir.dt.int32
U32 = mybir.dt.uint32
ALU = mybir.AluOpType
ACT = mybir.ActivationFunctionType
AX = mybir.AxisListType.X

P = 128
D = 1024
KD = D // P
NP, NS = 512, 32
T = NP + NS
HALF = T // 2
TT = NP // P + 1
SB, SL = 8, 4
PAST, PAGE = 256, 128
NPG = PAST // PAGE
RH, MH, DH = 4, 8, 64
G = 512
NE, NG, EPG = 32, 4, 8
CAP = 64
PAIRS = NE // 2
OVT = (2 * T) // CAP + 1
OVP = (OVT + 1) // 2
COLS = PAIRS + OVP
ALPHA = 2.0 ** 0.25
EPS = 1e-5
BIG = 1e30
GAMMAS = [1.0 - 2.0 ** (-5.0 - h) for h in range(RH)]

MK, RK, RV, RG, MV, MQ, RQ = range(7)
FM_OF = {MK: 0, RK: 1, MQ: 2, RQ: 3}

_CW = [("ident", P), ("before", P), ("ones", P), ("iota", P), ("dist", 512), ("slopes", MH),
       ("decay", RH * 512), ("kdec", RH * 4), ("sdecay", RH * NS), ("qdec_s", RH * NS), ("kdec_s", RH),
       ("bcol", SB * NS), ("brow", SB), ("headmask", 4 * MH), ("pastbias", PAST), ("newbias", SB // 2 * NS),
       ("i4", NG), ("i8", EPG), ("e64", NE), ("tokid", TT), ("valid", TT), ("iv", OVT), ("eps", 1)]
CO = {}
_o = 0
for _n, _w in _CW:
    CO[_n] = (_o, _w)
    _o += _w
NCONST = _o


def constants():
    c = np.zeros((P, NCONST), np.float64)

    def put(name, rows, val):
        o, w = CO[name]
        c[:rows, o:o + w] = np.asarray(val, np.float64).reshape(rows, w)

    p = np.arange(P)
    put("ident", P, np.eye(P))
    put("before", P, (p[:, None] < p[None, :]))
    put("ones", P, np.ones((P, P)))
    put("iota", P, np.tile(p, (P, 1)))
    d = np.arange(512)[None, :] - 384 - p[:, None]
    put("dist", P, np.where(d <= 0, d, -BIG))
    slopes = 2.0 ** (-8.0 * np.arange(1, MH + 1) / MH)
    put("slopes", P, np.tile(slopes, (P, 1)))
    lg = np.log(np.array(GAMMAS))
    ks = float(P) ** -0.5
    m = np.arange(512)[None, :] - p[:, None]
    put("decay", P, np.stack([np.where(m >= 0, ks * np.exp(g * np.maximum(m, 0)), 0) for g in lg], 1))
    put("kdec", P, np.stack([ks * np.exp(g * (NP - 1 - (np.arange(4)[None, :] * P + p[:, None]))) for g in lg], 1))
    j = np.arange(NS)
    same = (j[:, None] // SL == j[None, :] // SL)
    dt = (j[None, :] - j[:, None])
    put("sdecay", NS, np.stack([np.where(same & (dt >= 0), ks * np.exp(g * np.maximum(dt, 0)), 0) for g in lg], 1))
    put("qdec_s", P, np.tile(np.stack([np.exp(g * (j % SL + 1)) for g in lg], 0)[None], (P, 1, 1)))
    put("kdec_s", NS, np.stack([ks * np.exp(g * (SL - 1 - j % SL)) for g in lg], 1))
    put("bcol", P, np.tile((np.arange(SB)[:, None] == j[None, :] // SL)[None], (P, 1, 1)))
    put("brow", NS, (j[:, None] // SL == np.arange(SB)[None, :]))
    hp = np.arange(4)[None, :, None] * 2 + (p[:, None, None] // DH)
    put("headmask", P, (hp == np.arange(MH)[None, None, :]))
    q = np.arange(MH * SL)
    put("pastbias", 2 * MH * SL, np.tile(slopes[q // SL][:, None] * (np.arange(PAST)[None, :] - (PAST + q % SL)[:, None]),
                                        (2, 1)))
    nb = np.full((2, MH * SL, SB // 2, NS), -BIG)
    for b in range(SB):
        for k in range(SL):
            ok = q % SL >= k
            nb[b % 2, ok, b // 2, SL * b + k] = (slopes[q // SL] * (k - q % SL))[ok]
    put("newbias", 2 * MH * SL, nb)
    put("i4", P, np.tile(np.arange(NG), (P, 1)))
    put("i8", P, np.tile(np.arange(EPG), (P, 1)))
    put("e64", P, np.tile(CAP * np.arange(NE), (P, 1)))
    tok = p[:, None] + P * np.arange(TT)[None, :]
    put("tokid", P, np.where(tok < T, tok, 0))
    put("valid", P, tok < T)
    put("iv", P, np.tile(np.arange(OVT), (P, 1)))
    put("eps", P, np.full((P, 1), EPS))
    return c.astype(np.float32)


class Chain:

    def __init__(self, eng, sem):
        self.eng, self.sem, self.n = eng, sem, 0

    def mark(self, ins):
        ins.then_inc(self.sem, 1)
        self.n += 1
        return self.n

    def wait(self, value):
        self.eng.wait_ge(self.sem, value)

    def link(self, ins):
        self.wait(self.mark(ins))


def hybrid_step(nc, xT_d, x_d, w_tiles, w_out_d, w_router, b_router, b_merge, gn_g, ln1_g, ln1_b, ln2_g, ln2_b,
                experts_d, kT_pool, v_pool, page_table, state_d, const_d,
                y_prompt, y_sample, k_prompt, v_prompt, ret_prompt, k_sample, v_sample, ret_sample,
                x1_d, slots_d):
    with ExitStack() as ctx:
        def sb(name, shape, dt=F32):
            return ctx.enter_context(nc.sbuf_tensor(name, shape, dt))

        def sem(name):
            return ctx.enter_context(nc.semaphore(name))

        OM, TM = 0, 2560
        XT = TM + 5 * 2560
        FM = XT + KD * T
        RING = 5120
        EW = 3 * D
        ARENA = RING + 8 * EW
        WO = ARENA - 8 * D
        assert FM + 16 * T <= ARENA and WO >= FM
        arena = sb("arena", [P, ARENA])

        def tile3(base, a, b, rows=P):
            return arena[0:rows, base:base + a * b].rearrange("p (a b) -> p a b", a=a)

        om = tile3(OM, TT, G)
        tm = arena[:, TM:TM + 5 * 2560].rearrange("p (g t n) -> p g t n", g=5, t=TT)
        xT = tile3(XT, KD, T)
        fm = tile3(FM, 16, T)
        rk_t, rv_t, rg_t, mv_t = (tm[:, g] for g in (RK, RV, RG, MV))
        wo = tile3(WO, KD, D)
        x_tm = tile3(0, TT, D)

        def expert(s):
            return arena[:, RING + s * EW:RING + (s + 1) * EW]

        work = sb("work", [P, 2 * KD * T])
        merged = work[:, 0:KD * T].rearrange("p (k t) -> p k t", k=KD)
        kv_s = work[:, 4352:8448].rearrange("p (u m n) -> p u m n", u=2, m=2)
        oT = work[:, 4352:8704].rearrange("p (k t) -> p k t", k=KD)
        x1T = oT
        rst = work[:, 8448:8576]
        xg = work[:, 0:2048].rearrange("p (u n) -> p u n", u=2)
        xgT = work[:, 2048:4096].rearrange("p (u k t) -> p u k t", u=2, k=KD)
        yo = work[:, 4352:6400].rearrange("p (u n) -> p u n", u=2)
        sg = work[:, 6400:6656].rearrange("p (u s n) -> p u s n", u=2, s=2)
        hid = work[:, 6656:6912].rearrange("p (u s n) -> p u s n", u=2, s=2)
        picked = work[:, 0:8192].rearrange("p (u c n) -> p u c n", u=4, c=2)

        w_ring = sb("w_ring", [P, 4, D])
        cst = sb("cst", [P, NCONST])
        wr = sb("wr", [P, KD, NG + NE])
        br = sb("br", [P, NG + NE])
        bm = sb("bm", [P, 16])
        scratch = sb("scratch", [P, 5120])
        small = sb("small", [P, 2, 5])
        st_b = scratch[:, 0:1024].rearrange("p (u h v) -> p u h v", u=2, h=RH)
        rk_st = scratch[:, 1024:1536]
        k_st = scratch[:, 1536:2048].rearrange("p (t d) -> p t d", t=4)
        qz = scratch[:, 2048:3072].rearrange("p (u n) -> p u n", u=2)
        sd = scratch[:, 3072:4352]
        qbd = scratch[:, 4352:4608].rearrange("p (u c q) -> p u c q", u=2, c=4)
        qm = scratch[:, 4608:4864].rearrange("p (u h q) -> p u h q", u=2, h=RH)
        qds = scratch[:, 4864:4992].rearrange("p (h q) -> p h q", h=RH)
        sds = scratch[:, 4992:5120].rearrange("p (h q) -> p h q", h=RH)
        km = tile3(TM, 2, G, NS)
        SLOT_AT = [0, P, 3 * P, 6 * P, 10 * P]
        logit_s = w_ring[:, 2:4, :].rearrange("p a n -> p (a n)")
        pt_s = arena[:, TM + 1024:TM + 2560]
        spare = FM + 16 * T
        kds = arena[0:NS, spare + 512:spare + 1024]
        oTs = tile3(spare + 1024, KD, NS)
        zeros = work[:, D:2 * D]
        gng = work[:, 0:G]
        stage = scratch[:, 0:1088].rearrange("p (u t) -> p u t", u=2)
        sig_rg = om
        gb_s = scratch[:, 0:1088].rearrange("p (u t) -> p u t", u=2)
        t_b = scratch[:, 1088:2176].rearrange("p (u t) -> p u t", u=2)
        ln_g = scratch[:, 0:1024]
        ln_b = scratch[:, 1024:2048]
        logs = scratch[:, 2048:2048 + TT * 36].rearrange("p (t n) -> p t n", t=TT)
        rtr = scratch[:, 2304:5120]

        oh_lo = work[:, 0:2 * TT * P].rearrange("p (n q) -> p n q", n=2 * TT)
        oh_hi = work[:, 2 * TT * P:2 * TT * (P + COLS)].rearrange("p (n q) -> p n q", n=2 * TT)
        nmax, ssum = small[:, 0], small[:, 1]
        gstat = sb("gstat", [P, RH * TT, 6])
        gmv = sb("gmv", [P, RH * TT, 2])
        gstd = sb("gstd", [P, RH * TT])
        lst = sb("lst", [P, 2, 2, 6])
        lmv = sb("lmv", [P, 2, 2])
        lsd = sb("lsd", [P, 2 * TT])
        lsh = sb("lsh", [P, 2 * TT])
        wts = sb("wts", [P, 2, TT])
        slot_i = sb("slot_i", [P, 2, TT], I32)
        idx_i = sb("idx_i", [P, COLS], I32)
        idx_o = sb("idx_o", [P, 1], I32)
        ev_i = sb("ev_i", [1, 2 * OVP + 2], I32)
        pt_i = sb("pt_i", [1, SB * NPG], I32)

        ps = ctx.enter_context(nc.psum_tensor("ps", [P, 8, 512], F32))

        def C(name, rows=P):
            o, w = CO[name]
            return cst[0:rows, o:o + w]

        ident = C("ident")

        XQ = 4
        s_xT = [sem(f"xT_loaded{q}") for q in range(XQ)]
        s_id = sem("identity_loaded")
        s_w = [sem(f"w_tile_loaded{j}") for j in range(4)]
        s_par = sem("parameters_loaded")
        s_cst = sem("constants_loaded")
        s_pt = sem("page_table_loaded")
        s_kv = [sem(f"pages_loaded{u}") for u in range(2)]
        s_idle = sem("idle_written")
        s_zero = sem("zeros_made")
        s_z = sem("overflow_rows_cleared")
        s_rst = sem("head_state_stored")
        s_st = [sem(f"state_loaded{u}") for u in range(2)]
        s_sto = [sem(f"state_stored{u}") for u in range(2)]
        s_proj = sem("proj_done")
        s_pev = sem("proj_evacuated")
        s_tr = sem("group_transposed")
        s_trd = sem("token_major_written")
        s_fmc = sem("feature_major_copied")
        s_kst = sem("k_stored")
        s_out = sem("outputs_stored")
        s_sig = sem("rg_sigmoid")
        s_rg = sem("rg_gated")
        dve_c = sem("dve_chain")
        pool_c = sem("pool_chain")
        act_c = sem("act_chain")
        s_gh = sem("gate_half_done")
        s_ghe = sem("gate_half_evacuated")
        s_s = sem("scores_ready")
        s_su = sem("scores_used")
        s_max = sem("logits_ready")
        s_exp = sem("exp_done")
        s_inv = sem("sums_inverted")
        s_pn = sem("sample_probs_ready")
        s_t = sem("probs_transposed")
        s_tu = sem("probs_copied")
        s_o = sem("products_ready")
        s_ou = sem("products_used")
        s_stg = sem("staged")
        s_ret = sem("retention_state_ready")
        s_cross = sem("sample_retention_ready")
        s_gst = sem("group_stats_ready")
        s_gsq = sem("group_std_ready")
        s_gn = sem("branch_rows_ready")
        s_ot = sem("branch_transposed")
        s_otc = sem("branch_copied")
        s_gas = sem("first_gate_ready")
        s_cg = sem("second_gate_projected")
        s_cgs = sem("second_gate_ready")
        s_cb = sem("branches_done")
        s_cbu = sem("branches_used")
        s_mg = sem("merged_ready")
        s_wo = sem("w_out_loaded")
        s_x = sem("x_loaded")
        s_ln1 = sem("ln1_loaded")
        s_ln2 = sem("ln2_loaded")
        s_y = sem("y_done")
        s_yu = sem("y_used")
        s_var = sem("variance_ready")
        s_std = sem("std_ready")
        s_x1 = sem("x1_ready")
        s_x1s = sem("x1_stored")
        s_x1t = sem("x1_transposed")
        s_x1c = sem("x1_copied")
        s_lg = sem("router_logits_ready")
        s_lgu = sem("router_logits_used")
        s_gexp_i = sem("router_exp_in")
        s_gexp = sem("router_exp_done")
        s_msk = sem("selection_ready")
        s_pre = sem("ranks_ready")
        s_oh = sem("slot_onehots_ready")
        s_ohu = sem("slot_onehots_used")
        s_idx = sem("slot_tokens_ready")
        s_nov = sem("overflow_count_ready")
        s_e = [sem(f"expert_loaded{s}") for s in range(8)]
        s_gx = [sem(f"tokens_gathered{u}") for u in range(2)]
        s_xt = sem("tokens_transposed")
        s_xc = sem("tokens_copied")
        s_gu = sem("gate_up_done")
        s_sl = sem("silu_done")
        s_h = sem("hidden_ready")
        s_dn = sem("down_done")
        s_ye = sem("expert_rows_evacuated")
        s_ys = [sem(f"expert_rows_stored{u}") for u in range(2)]
        s_ovi = sem("overflow_index_ready")
        s_ovg = sem("overflow_gathered")
        s_ovw = sem("overflow_weights")
        s_ovs = sem("overflow_stored")
        s_yg = [sem(f"rows_gathered{u}") for u in range(4)]
        s_xa = sem("x1_scaled")
        s_shift = sem("row_shift_ready")
        s_nrm = sem("rows_normalised")
        s_gain = sem("rows_scaled")
        s_fin = sem("final_ready")
        s_fru = sem("rows_used")

        block = ctx.enter_context(nc.Block())

        idle = sb("idle", [P, 1])
        dgl = sb("dgl", [P, TT, NG])[:]
        dm = sb("dm", [P, TT])[:]
        lohi = sb("lohi", [P, 2, 2, TT], I32)

        def M(u, qb):
            return ("moba", u, qb)

        SAMP = ("samp",)
        ORDER = [("S", M(0, 0)), ("S", M(0, 1)), ("G", 0),
                 ("S", M(0, 2)), ("T", M(0, 0)), ("S", ("ret", 0)), ("O", M(0, 0)),
                 ("S", M(0, 3)), ("T", M(0, 1)), ("S", ("ret", 1)), ("O", M(0, 1)),
                 ("S", ("samp", 0)), ("T", M(0, 2)), ("S", ("samp", 1)), ("O", M(0, 2)), ("S", ("ret", 2)),
                 ("O", ("skv", 0)),
                 ("S", M(1, 0)), ("T", M(0, 3)), ("S", ("ret", 3)), ("O", M(0, 3)), ("G", 1),
                 ("S", M(1, 1)), ("N", SAMP), ("T", SAMP), ("O", ("skv", 1)), ("O", ("samp", 0)), ("O", ("samp", 1)),
                 ("S", M(1, 2)), ("T", M(1, 0)), ("O", ("reto",)), ("O", M(1, 0)),
                 ("S", M(1, 3)), ("T", M(1, 1)), ("O", ("rets",)), ("O", M(1, 1)),
                 ("G", 2), ("T", M(1, 2)), ("G", 3), ("T", M(1, 3)), ("O", M(1, 2)), ("O", M(1, 3))]
        KT_OFF = [0, 512, 896, 1152]

        def places(kind):
            return {jb: n for n, jb in enumerate([jb for k, jb in ORDER if k == kind])}

        S_IDX, T_IDX, O_IDX = places("S"), places("T"), places("O")
        nS, nT, nO = len(S_IDX), len(T_IDX), len(O_IDX)
        INV_IDX = {jb: n for n, jb in enumerate([jb for k, jb in ORDER if k == "N" or k == "O" and jb[0] == "moba"])}
        assert nS % 2 == 0 and nO % 2 == 0

        def slot(jb):
            return jb[2] if jb[0] == "moba" else 4

        def before_in_slot(i, jb, idx, n):
            if jb[0] == "moba" and jb[1] == 1:
                return n * i + n + idx[M(0, jb[2])] + 1
            return n * i + idx[M(1, jb[2]) if jb[0] == "moba" else jb] + 1

        def logit(jb, w, rows=P):
            return logit_s[0:rows, SLOT_AT[slot(jb)]:SLOT_AT[slot(jb)] + w]

        def pt(jb, w):
            return pt_s[:, SLOT_AT[slot(jb)]:SLOT_AT[slot(jb)] + w]

        SBANK, TBANK, OBANK, XBANK = 2, 4, 5, 7

        def s_bank(jb):
            return SBANK + S_IDX[jb] % 2

        def o_bank(jb):
            return OBANK + O_IDX[jb] % 2

        def wg(s, k):
            return expert(s)[:, k * P:(k + 1) * P]

        def wu(s, k):
            return expert(s)[:, D + k * P:D + (k + 1) * P]

        def wd(s, half):
            return expert(s)[:, 2 * D + half * 512:2 * D + (half + 1) * 512]

        @block.sync
        def _(sp):
            def w_tile(n):
                return w_tiles[bass.ds(n, 1)] if not isinstance(n, int) else w_tiles[n]

            for j in range(4):
                sp.dma_start(w_ring[:, j, :], w_tile(j)).then_inc(s_w[j], 16)
                if j == 1:
                    sp.dma_start(cst[:, P:NCONST], const_d[:, P:NCONST]).then_inc(s_cst, 16)
            with sp.Fori(1, 7) as i:
                for j in range(4):
                    sp.wait_ge(s_proj, 4 * i + j - 3)
                    sp.dma_start(w_ring[:, j, :], w_tile(4 * i + j)).then_inc(s_w[j], 16)
            kp = k_prompt.rearrange("d b (t p) h e -> p (d b t) (h e)", p=P)
            vp = v_prompt.rearrange("d b (t p) h e -> p (d b t) (h e)", p=P)
            ks_ = k_sample.rearrange("d b l h e -> (d b l) (h e)")
            vs_ = v_sample.rearrange("d b l h e -> (d b l) (h e)")
            sp.wait_ge(s_trd, 2 + 4)
            sp.dma_start(kp, tm[:, MK, 0:4, :]).then_inc(s_kst, 16)
            sp.dma_start(ks_, tm[0:NS, MK, 4, :]).then_inc(s_kst, 16)
            sp.wait_ge(s_trd, 2 + 20)
            sp.dma_start(vp, tm[:, MV, 0:4, :]).then_inc(s_out, 16)
            sp.dma_start(vs_, tm[0:NS, MV, 4, :]).then_inc(s_out, 16)
            stv = state_d.rearrange("d b h k v -> k (d b) h v")
            sto = ret_sample.rearrange("d b h k v -> k (d b) h v")

            def pages(b, u):
                for pg in range(NPG):
                    r = sp.value_load(pt_i[0:1, bass.ds(b * NPG + pg, 1)], min_val=0, max_val=kT_pool.shape[0] - 1)
                    sp.dma_start(kv_s[:, u, 0, :].rearrange("p (c t) -> p c t", c=4)[:, :, pg * PAGE:(pg + 1) * PAGE],
                                 kT_pool[bass.ds(r, 1)].rearrange("o c p t -> p (o c) t")).then_inc(s_kv[u], 16)
                    sp.dma_start(kv_s[:, u, 1, pg * 512:(pg + 1) * 512],
                                 v_pool[bass.ds(r, 1)].rearrange("o p n -> p (o n)")).then_inc(s_kv[u], 16)

            sp.wait_ge(s_pt, 16)
            for u in range(2):
                sp.wait_ge(s_proj, 25 + u)
                sp.dma_start(w_ring[:, u, :], w_tile(28 + u)).then_inc(s_w[u], 16)
                pages(u, u)
            sp.wait_ge(s_fmc, 10)
            sp.wait_ge(s_tr, 2 + 20)
            for u in range(2):
                sp.dma_start(st_b[:, u], stv[:, u]).then_inc(s_st[u], 16)
            rpv = ret_prompt.rearrange("d b h k v -> (d b h) k v")

            def store_pass(i, refill):
                for u in range(2):
                    sp.wait_ge(s_ou, nO * i + 2 + O_IDX[("skv", u)] + 1)
                    sp.dma_start(sto[:, bass.ds(2 * i + u, 1)].rearrange("k o h v -> k (o h) v"),
                                 st_b[:, u]).then_inc(s_sto[u], 16)
                if refill:
                    sp.wait_ge(s_gh, 4 * i + 2)
                    sp.dma_start(w_ring[:, 0, :], w_tile(30 + 2 * i)).then_inc(s_w[0], 16)
                    for u in range(2):
                        sp.wait_ge(s_sto[u], 16 * (i + 1))
                        sp.dma_start(st_b[:, u], stv[:, bass.ds(2 * i + 2 + u, 1)].rearrange("k o h v -> k (o h) v")
                                     ).then_inc(s_st[u], 16)
                        sp.wait_ge(s_o, nO * i + nO + O_IDX[("samp", u)] + 1)
                        pages(2 * i + 2 + u, u)
                sp.wait_ge(s_ou, nO * i + 2 + O_IDX[("rets",)] + 1)
                sp.dma_start(rpv[bass.ds(i, 1)].rearrange("o k v -> (o k) v"), rst).then_inc(s_rst, 16)
                if refill:
                    sp.wait_ge(s_gh, 4 * i + 4)
                    sp.dma_start(w_ring[:, 1, :], w_tile(31 + 2 * i)).then_inc(s_w[1], 16)

            with sp.Fori(0, 3) as i:
                store_pass(i, True)
            store_pass(3, False)
            for u in range(2):
                sp.wait_ge(s_gh, 14 + 2 * u)
                sp.dma_start(w_ring[:, u, :], w_tile(36 + u)).then_inc(s_w[u], 16)
            sp.wait_ge(s_t, 5 * nT)
            for u in range(2):
                sp.dma_start(w_ring[:, 2 + u, :], w_tile(38 + u)).then_inc(s_w[2 + u], 16)
            def refill_slices(i):
                for u in range(2):
                    sp.wait_ge(s_cg, 2 * i + u - 1)
                    sp.dma_start(w_ring[:, 2 * u, :], w_tile(36 + 4 * i + 2 * u)).then_inc(s_w[2 * u], 16)
                    sp.wait_ge(s_cb, 2 * i + u - 1)
                    sp.dma_start(w_ring[:, 2 * u + 1, :], w_tile(37 + 4 * i + 2 * u)).then_inc(s_w[2 * u + 1], 16)

            refill_slices(1)
            sp.wait_ge(s_otc, 2 * TT)
            sp.dma_start(wo, w_out_d.rearrange("(k p) n -> p k n", p=P)).then_inc(s_wo, 16)
            sp.wait_ge(s_kst, 32)
            sp.dma_start(x_tm[:, 0:4, :], x_d[0:NP].rearrange("(t p) n -> p t n", p=P)).then_inc(s_x, 16)
            sp.dma_start(x_tm[0:NS, 4, :], x_d[NP:T]).then_inc(s_x, 16)
            with sp.Fori(2, 4) as i:
                refill_slices(i)
            for s in range(3):
                sp.dma_start(expert(s), experts_d[s]).then_inc(s_e[s], 16)
            sp.wait_ge(s_cg, 8)
            for s in (3, 4):
                sp.dma_start(expert(s), experts_d[s]).then_inc(s_e[s], 16)
            sp.wait_ge(s_mg, 10)
            sp.dma_start(ln_g, ln1_g.partition_broadcast(P)).then_inc(s_ln1, 16)
            sp.dma_start(ln_b, ln1_b.partition_broadcast(P)).then_inc(s_ln1, 16)
            for t in range(TT):
                sp.wait_ge(s_x1, t + 1)
                rows = P if t < 4 else NS
                sp.dma_start(x1_d[t * P:t * P + rows], x_tm[0:rows, t, :]).then_inc(s_x1s, 16)
            sp.wait_ge(s_y, TT)
            for s in (5, 6, 7):
                sp.dma_start(expert(s), experts_d[s]).then_inc(s_e[s], 16)
            sp.dma_start(ln_g, ln2_g.partition_broadcast(P)).then_inc(s_ln2, 16)
            sp.dma_start(ln_b, ln2_b.partition_broadcast(P)).then_inc(s_ln2, 16)
            yv = slots_d.rearrange("(c p) n -> c p n", p=P)

            def store_pair(n, u):
                sp.wait_ge(s_ye, n + 3)
                sp.dma_start(yv[bass.ds(n, 1)].rearrange("o p n -> (o p) n"), yo[:, u]).then_inc(s_ys[u], 16)

            with sp.Fori(0, 3) as i:
                for q in range(4):
                    store_pair(4 * i + q, q % 2)
                    sp.wait_ge(s_dn, 4 * i + q + 1)
                    for s in (2 * q, 2 * q + 1):
                        sp.dma_start(expert(s), experts_d[bass.ds(8 * i + 8 + s, 1)].rearrange("o p n -> (o p) n")
                                     ).then_inc(s_e[s], 16)
            for q in range(4):
                store_pair(12 + q, q % 2)
            sp.wait_ge(s_nov, 1)
            nov = sp.value_load(ev_i[0:1, 2 * OVP:2 * OVP + 1], min_val=0, max_val=OVP)
            with sp.If(nov > 0):
                with sp.Fori(0, nov) as i:
                    sp.wait_ge(s_dn, PAIRS + i)
                    for s in range(2):
                        e = sp.value_load(ev_i[0:1, bass.ds(2 * i + s, 1)], min_val=0, max_val=NE - 1)
                        sp.dma_start(expert(s), experts_d[bass.ds(e, 1)].rearrange("o p n -> (o p) n")
                                     ).then_inc(s_ovw, 16)
                    sp.wait_ge(s_ye, PAIRS + i + 3)
                    sp.dma_start(yv[bass.ds(PAIRS + i, 1)].rearrange("o p n -> (o p) n"), yo[:, 0]).then_inc(s_ovs, 16)
            for t in range(TT):
                sp.wait_ge(s_fin, t + 1)
                if t < 4:
                    sp.dma_start(y_prompt[0, t * P:(t + 1) * P, :], x_tm[:, t, :]).then_inc(s_out, 16)
                else:
                    sp.dma_start(y_sample.rearrange("b l n -> (b l) n"), x_tm[0:NS, t, :]).then_inc(s_out, 16)
            sp.wait_ge(s_sto[0], 64)
            sp.wait_ge(s_sto[1], 64)
            sp.wait_ge(s_x1s, 16 * TT)
            sp.wait_ge(s_rst, 80)
            sp.wait_ge(s_out, 16 * (2 + TT))

        @block.tensor
        def _(pe):
            mm = nc.tensor.matmul

            def tr(out, in_, rows):
                return nc.tensor.transpose(out, in_, ident[0:rows, 0:rows])

            def project_half(slot, bank, half, first=False):
                for k in range(KD):
                    if first and k % (KD // XQ) == 0:
                        pe.wait_ge(s_xT[k // (KD // XQ)], 16)
                    m = mm(ps[:, bank, 0:HALF], w_ring[:, slot, k * P:(k + 1) * P],
                           xT[:, k, half * HALF:(half + 1) * HALF], start=k == 0, stop=k == KD - 1)
                return m

            pe.sem_inc(s_tr, 2)
            pe.sem_inc(s_s, nS)
            pe.sem_inc(s_t, nT)
            pe.sem_inc(s_o, nO)
            pe.sem_inc(s_gu, 1)

            def group(i, token_major):
                for j in range(4):
                    n = 4 * i + j
                    pe.wait_ge(s_w[j], 16 * (i + 1))
                    pe.wait_ge(s_pev, n + 1)
                    project_half(j, 2 * (j % 2), 0, first=j == 0 and token_major)
                    project_half(j, 2 * (j % 2) + 1, 1).then_inc(s_proj, 1)
                    if token_major:
                        if j > 0:
                            turn(n - 1, j - 1)
                if token_major:
                    turn(4 * i + 3, 3)

            def turn(n, j):
                pe.wait_ge(s_pev, n + 3)
                pe.wait_ge(s_trd, n + 1)
                pe.wait_ge(s_id, 16)
                b = 4 + 2 * (j % 2)
                for t in range(4):
                    tr(ps[:, b, t * P:(t + 1) * P], stage[:, j % 2, t * P:(t + 1) * P], P)
                tr(ps[0:NS, b + 1, 0:P], stage[:, j % 2, NP:T], P).then_inc(s_tr, 1)

            with pe.Fori(0, 5) as i:
                group(i, True)
            with pe.Fori(5, 7) as i:
                group(i, False)

            pe.wait_ge(s_pev, 30)
            pe.wait_ge(s_trd, 22)
            for h in range(RH):
                m = mm(ps[0:NS, SBANK, h * NS:(h + 1) * NS], fm[:, 4 * FM_OF[RK] + h, NP:T],
                       fm[:, 4 * FM_OF[RQ] + h, NP:T], start=True, stop=True)
            m.then_inc(s_cross, 1)
            pe.wait_ge(s_ret, 1)
            for h in range(RH):
                mm(ps[0:NS, XBANK, h * P:(h + 1) * P], sds[0:NS, h, :], rv_t[0:NS, 4, h * P:(h + 1) * P],
                   start=h == 0, stop=False, skip_group_check=True)

            def gate_half(i, q):
                u, half = q // 2, q % 2
                if half == 0:
                    pe.wait_ge(s_w[u], 16 * (7 + i + 1))
                pe.wait_ge(s_ghe, 4 * i + q + 1)
                project_half(u, q % 2, half).then_inc(s_gh, 1)

            with pe.Fori(0, 4) as i:
                def scores(jb):
                    k = S_IDX[jb]
                    b = s_bank(jb)
                    pe.wait_ge(s_su, nS * i + k + 1)
                    if jb[0] == "moba":
                        _, u, qb = jb
                        if qb == 0:
                            pe.wait_ge(s_stg, 6 * i + [1, 6][u])
                        m = mm(ps[:, b, 0:P * (qb + 1)], qz[:, u, qb * P:(qb + 1) * P],
                               fm[:, bass.ds(i, 1), 0:P * (qb + 1)].rearrange("p o n -> p (o n)"),
                               start=True, stop=True)
                    elif jb[0] == "ret":
                        kb = jb[1]
                        if kb == 0:
                            pe.wait_ge(s_stg, 6 * i + 2)
                        w = NP - kb * P
                        m = mm(ps[:, b, 0:w], rk_st[:, kb * P:(kb + 1) * P],
                               fm[:, bass.ds(4 * FM_OF[RQ] + i, 1), kb * P:NP].rearrange("p o n -> p (o n)"),
                               start=True, stop=True)
                    else:
                        u = jb[1]
                        pe.wait_ge(s_stg, 6 * i + 3 + u)
                        pe.wait_ge(s_kv[u], 64 * (i + 1))
                        for c in range(4):
                            mm(ps[NS * u:NS * (u + 1), b, 0:PAST], qbd[:, u, c, :], kv_s[:, u, 0, c * PAST:(c + 1) * PAST],
                               start=c == 0, stop=c == 3)
                        for c in range(4):
                            m = mm(ps[NS * u:NS * (u + 1), b, PAST:PAST + NS], qbd[:, u, c, :],
                                   fm[:, 4 * FM_OF[MK] + c, NP:T], start=c == 0, stop=c == 3)
                    m.then_inc(s_s, 1)

                def turns(jb):
                    t = T_IDX[jb]
                    if jb[0] == "moba":
                        pe.wait_ge(s_exp, nT * i + t + 1)
                    else:
                        pe.wait_ge(s_pn, i + 1)
                    pe.wait_ge(s_tu, nT * i + t + 1)
                    for kb in range(jb[2] + 1 if jb[0] == "moba" else NPG + 1):
                        m = tr(ps[:, TBANK, kb * P:(kb + 1) * P], logit(jb, 4 * P)[:, kb * P:(kb + 1) * P], P)
                    m.then_inc(s_t, 1)

                def products(jb):
                    k = O_IDX[jb]
                    b = o_bank(jb)
                    pe.wait_ge(s_ou, nO * i + k + 1)
                    if jb[0] in ("moba", "samp"):
                        tj = jb if jb[0] == "moba" else SAMP
                        pe.wait_ge(s_tu, nT * i + T_IDX[tj] + 2)
                    if jb[0] == "moba":
                        _, u, qb = jb
                        for kb in range(qb + 1):
                            m = mm(ps[:, b, 0:DH], pt(jb, 4 * P)[:, kb * P:(kb + 1) * P],
                                   mv_t[:, kb, bass.ds((2 * i + u) * DH, DH)], start=kb == 0, stop=kb == qb)
                    elif jb[0] == "samp":
                        u = jb[1]
                        pr = pt(SAMP, 3 * 2 * NS).rearrange("p (k q) -> p k q", k=3)[:, :, u * NS:(u + 1) * NS]
                        for c in range(4):
                            o = ps[:, b, 8 * c:8 * c + 8]
                            for pg in range(NPG):
                                mm(o, kv_s[:, u, 1, pg * 512 + c * P:pg * 512 + (c + 1) * P],
                                   pr[:, pg, 8 * c:8 * c + 8], start=pg == 0, stop=False)
                            m = mm(o, mv_t[0:NS, 4, c * P:(c + 1) * P], pr[0:NS, NPG, 8 * c:8 * c + 8],
                                   start=False, stop=True)
                    elif jb[0] == "skv":
                        u = jb[1]
                        for h in range(RH):
                            if h == 0:
                                pe.wait_ge(s_st[u], 16 * (i + 1))
                            x = mm(ps[0:NS, XBANK, h * P:(h + 1) * P], qm[:, u, h, :], st_b[:, u, h, :],
                                   start=False, stop=False, skip_group_check=True)
                        x.then_inc(s_cross, 1)
                        for h in range(RH):
                            m = mm(ps[:, b, h * P:(h + 1) * P], km[0:NS, u, h * P:(h + 1) * P],
                                   rv_t[0:NS, 4, h * P:(h + 1) * P], start=True, stop=True)
                    elif jb[0] == "reto":
                        pe.wait_ge(s_su, nS * i + 2 + S_IDX[("ret", 3)] + 1)
                        for qb in range(4):
                            for kb in range(qb + 1):
                                o = KT_OFF[kb] + (qb - kb) * P
                                m = mm(ps[:, b, qb * P:(qb + 1) * P], sd[:, o:o + P],
                                       rv_t[:, kb, bass.ds(i * P, P)], start=kb == 0, stop=kb == qb)
                    else:
                        pe.wait_ge(s_stg, 6 * i + 5)
                        for kb in range(4):
                            m = mm(ps[:, b, 0:P], k_st[:, kb, :], rv_t[:, kb, bass.ds(i * P, P)],
                                   start=kb == 0, stop=kb == 3)
                    m.then_inc(s_o, 1)

                for kind, jb in ORDER:
                    if kind == "S":
                        scores(jb)
                    elif kind == "T":
                        turns(jb)
                    elif kind == "O":
                        products(jb)
                    elif kind == "G":
                        gate_half(i, jb)

            def second_gate(turn_, n, u):
                pe.wait_ge(s_w[2 * u], 16 * ([11, 7][u] + turn_ + 1))
                pe.wait_ge(s_cgs, n + 1)
                project_half(2 * u, 2 * u, 0)
                project_half(2 * u, 2 * u + 1, 1).then_inc(s_cg, 1)

            pe.wait_ge(s_ghe, 18)
            pe.wait_ge(s_su, nS * 4 + 2)
            for u in range(2):
                second_gate(0, u, u)
            pe.wait_ge(s_tu, 4 * nT + 1)
            pe.wait_ge(s_ou, nO * 4 + 2)
            for t in range(TT):
                r = P if t < 4 else NS
                pe.wait_ge(s_gn, t + 1)
                if t >= 2:
                    pe.wait_ge(s_otc, 2 * t - 3)
                b = 4 + 2 * (t % 2)
                for c in range(4):
                    m = tr(ps[:, b, c * P:c * P + r], rg_t[0:r, t, c * P:(c + 1) * P], r)
                m.then_inc(s_ot, 1)
                if t < 4:
                    if t >= 2:
                        pe.wait_ge(s_otc, 2 * t - 2)
                    for c in range(4):
                        m = tr(ps[:, b + 1, c * P:(c + 1) * P], om[:, t, c * P:(c + 1) * P], P)
                    m.then_inc(s_ot, 1)
            pe.wait_ge(s_otc, 2 * TT)

            def branches(i, u):
                pe.wait_ge(s_w[2 * u + 1], 16 * ([11, 7][u] + i + 1))
                pe.wait_ge(s_cbu, 2 * i + u + 1)
                for br_ in range(2):
                    for half in range(2):
                        for k in range(4):
                            kk = 4 * br_ + k
                            m = mm(ps[:, 4 + 2 * br_ + half, 0:HALF], w_ring[:, 2 * u + 1, kk * P:(kk + 1) * P],
                                   oT[:, kk, half * HALF:(half + 1) * HALF], start=k == 0, stop=k == 3)
                m.then_inc(s_cb, 1)

            with pe.Fori(0, 3) as i:
                for u in range(2):
                    branches(i, u)
                    second_gate(i + 1, 2 * i + u + 2, u)
            for u in range(2):
                branches(3, u)

            def router(t):
                r = P if t < 4 else NS
                pe.wait_ge(s_x1, t + 1)
                pe.wait_ge(s_x1c, t)
                for k in range(KD):
                    m = tr(ps[:, 4 + k // 4, (k % 4) * P:(k % 4) * P + r], x_tm[0:r, t, k * P:(k + 1) * P], r)
                m.then_inc(s_x1t, 1)
                pe.wait_ge(s_x1c, t + 1)
                for k in range(KD):
                    m = mm(ps[0:r, 6, t * 36:(t + 1) * 36], x1T[:, k, t * P:t * P + r], wr[:, k, :],
                           start=k == 0, stop=k == KD - 1)
                m.then_inc(s_lg, 1)

            pe.wait_ge(s_wo, 16)
            pe.wait_ge(s_mg, 10)
            pe.wait_ge(s_cgs, 10)
            for t in range(TT):
                r = P if t < 4 else NS
                if t >= 2:
                    pe.wait_ge(s_yu, t - 1)
                for half in range(2):
                    for k in range(KD):
                        m = mm(ps[0:r, 2 * (t % 2) + half, :], merged[:, k, t * P:t * P + r],
                               wo[:, k, half * 512:(half + 1) * 512], start=k == 0, stop=k == KD - 1)
                m.then_inc(s_y, 1)
                if t > 0:
                    router(t - 1)
            router(TT - 1)
            pe.wait_ge(s_cbu, 9)
            pe.wait_ge(s_msk, 1)
            sel = rtr[:, 0:TT * NE].rearrange("p (t e) -> p t e", t=TT)
            rank_of = ps[:, 7, 0:(TT + 1) * NE].rearrange("p (t e) -> p t e", t=TT + 1)
            mm(rank_of[:, 0], C("before"), sel[:, 0], start=True, stop=True)
            for s in range(TT):
                mm(rank_of[:, s + 1:TT + 1], C("ones"), sel[:, s:s + 1].to_broadcast([P, TT - s, NE]),
                   start=s == 0, stop=False, skip_group_check=True)
            mm(rank_of[:, 1:TT], C("before"), sel[:, 1:TT], start=False, stop=True, skip_group_check=True
               ).then_inc(s_pre, 1)
            for n in range(2 * TT):
                if n % TT == 0:
                    pe.wait_ge(s_oh, n // TT + 1)
                m = mm(ps[:, 6, 256:256 + COLS], oh_lo[:, n], oh_hi[:, n], start=n == 0, stop=n == 2 * TT - 1)
            m.then_inc(s_ohu, 1)

            def turn_tokens(n, u, par):
                pe.wait_ge(s_gx[u], par)
                pe.wait_ge(s_xc, n)
                for k in range(KD):
                    m = tr(ps[:, k // 4, (k % 4) * P:(k % 4 + 1) * P], xg[:, u, k * P:(k + 1) * P], P)
                m.then_inc(s_xt, 1)

            def gate_up(s0, u, loaded):
                for s in range(2):
                    pe.wait_ge(*loaded(s0 + s))
                    for m_, w in enumerate((wg, wu)):
                        for k in range(KD):
                            m = mm(ps[:, 2 + u, (2 * s + m_) * CAP:(2 * s + m_ + 1) * CAP], w(s0 + s, k),
                                   xgT[:, u, k, s * CAP:(s + 1) * CAP], start=k == 0, stop=k == KD - 1)
                m.then_inc(s_gu, 1)

            def down(s0, u):
                for s in range(2):
                    for half in range(2):
                        m = mm(ps[s * CAP:(s + 1) * CAP, 4 + 2 * u + half, :], hid[:, u, s, :], wd(s0 + s, half),
                               start=True, stop=True)
                m.then_inc(s_dn, 1)

            pe.wait_ge(s_x1c, TT)
            pe.wait_ge(s_idx, 1)
            turn_tokens(0, 0, 16)
            with pe.Fori(0, 4) as i:
                for q in range(4):
                    n, u = 4 * i + q, q % 2
                    pe.wait_ge(s_xc, n + 1)
                    gate_up(2 * q, u, lambda s: (s_e[s], 16 * (i + 1)))
                    turn_tokens(n + 1, 1 - u, 16 * (2 * i + (q + 1) // 2 + 1))
                    pe.wait_ge(s_h, n + 2)
                    pe.wait_ge(s_ye, n + 1)
                    down(2 * q, u)
            pe.wait_ge(s_nov, 1)
            nov = pe.value_load(ev_i[0:1, 2 * OVP:2 * OVP + 1], min_val=0, max_val=OVP)
            with pe.If(nov > 0):
                with pe.Fori(0, nov) as i:
                    pe.wait_ge(s_ovg, 16 * (i + 1))
                    pe.wait_ge(s_xc, PAIRS + 1 + i)
                    for k in range(KD):
                        m = tr(ps[:, k // 4, (k % 4) * P:(k % 4 + 1) * P], xg[:, 0, k * P:(k + 1) * P], P)
                    m.then_inc(s_xt, 1)
                    pe.wait_ge(s_xc, PAIRS + 2 + i)
                    gate_up(0, 0, lambda s: (s_ovw, 32 * (i + 1)))
                    pe.wait_ge(s_h, PAIRS + 2 + i)
                    pe.wait_ge(s_ye, PAIRS + i + 2)
                    down(0, 0)

        @block.scalar
        def _(act):
            A = nc.scalar.activation
            for q in range(XQ):
                act.dma_start(xT[:, q * KD // XQ:(q + 1) * KD // XQ, :], xT_d[:, q * KD // XQ:(q + 1) * KD // XQ, :]
                              ).then_inc(s_xT[q], 16)
            act.dma_start(ident, const_d[:, 0:P]).then_inc(s_id, 16)
            act.dma_start(pt_i[:], page_table).then_inc(s_pt, 16)
            act.dma_start(bm[:], b_merge).then_inc(s_par, 16)
            act.dma_start(gng, gn_g.partition_broadcast(P)).then_inc(s_par, 16)
            act.dma_start(wr[:], w_router).then_inc(s_par, 16)
            act.dma_start(br[:], b_router.partition_broadcast(P)).then_inc(s_par, 16)
            act.wait_ge(s_zero, 1)
            act.dma_start(slots_d.rearrange("(c p) n -> p c n", p=P)[:, PAIRS:COLS, :],
                          zeros.unsqueeze(1).to_broadcast([P, OVP, D])).then_inc(s_z, 16)
            act.sem_inc(s_pev, 2)
            act.sem_inc(s_ghe, 2)
            act.sem_inc(s_cgs, 2)
            act.sem_inc(s_tu, 1)

            def to_stage(i, copied):
                for j in range(4):
                    n = 4 * i + j
                    act.wait_ge(s_proj, n + 1)
                    act.wait_ge(s_tr, n + 1)
                    if copied:
                        act.wait_ge(s_fmc, n + 1)
                    A(stage[:, j % 2].rearrange("p (h c) -> p h c", h=2), ps[:, 2 * (j % 2):2 * (j % 2) + 2, 0:HALF],
                      ACT.Identity).then_inc(s_pev, 1)

            with act.Fori(0, 2) as i:
                to_stage(i, True)
            act.wait_ge(s_fmc, 10)
            with act.Fori(2, 5) as i:
                to_stage(i, False)
            act.wait_ge(s_trd, 2 + 16)
            A(sig_rg[:, 0:4, :], rg_t[:, 0:4, :], ACT.Sigmoid)
            A(sig_rg[0:NS, 4, :], rg_t[0:NS, 4, :], ACT.Sigmoid).then_inc(s_sig, 1)
            for g in (MQ, RQ):
                for j in range(4):
                    act.wait_ge(s_proj, 4 * g + j + 1)
                    A(fm[:, 4 * FM_OF[g] + j, :].rearrange("p (h c) -> p h c", h=2),
                      ps[:, 2 * (j % 2):2 * (j % 2) + 2, 0:HALF], ACT.Identity,
                      scale=DH ** -0.5 if g == MQ else 1.0).then_inc(s_pev, 1)

            act.wait_ge(s_par, 64)
            act.wait_ge(s_z, 16)
            act.wait_ge(s_rg, 1)
            with act.Fori(0, 4) as i:
                def gate_copy(q):
                    u, half = q // 2, q % 2
                    act.wait_ge(s_gh, 4 * i + q + 1)
                    A(merged[:, bass.ds(2 * i + u, 1), half * HALF:(half + 1) * HALF].rearrange("p o n -> p (o n)"),
                      ps[:, q % 2, 0:HALF], ACT.Identity, bias=bm[:, bass.ds(2 * i + u, 1)]).then_inc(s_ghe, 1)

                def probs(jb):
                    t = T_IDX[jb]
                    act.wait_ge(s_max, nT * i + t + 1)
                    r, w = (P, P * (jb[2] + 1)) if jb[0] == "moba" else (2 * NS, PAST + NS)
                    s_ = slot(jb)
                    A(logit(jb, w, r), logit(jb, w, r), ACT.Exp, bias=nmax[0:r, s_:s_ + 1],
                      accum_out=ssum[0:r, s_:s_ + 1]).then_inc(s_exp, 1)

                def copy_probs(jb):
                    act.wait_ge(s_t, nT * i + nT + T_IDX[jb] + 1)
                    if jb[0] == "moba":
                        act.wait_ge(s_o, before_in_slot(i, jb, O_IDX, nO))
                        w = P * (jb[2] + 1)
                        A(pt(jb, w), ps[:, TBANK, 0:w], ACT.Identity).then_inc(s_tu, 1)
                    else:
                        act.wait_ge(s_o, nO * i + O_IDX[("samp", 1)] + 1)
                        A(pt(jb, 6 * NS).rearrange("p (k q) -> p k q", k=3),
                          ps[:, TBANK, 0:3 * P].rearrange("p (k q) -> p k q", k=3)[:, :, 0:2 * NS],
                          ACT.Identity).then_inc(s_tu, 1)

                waiting = []
                for kind, jb in ORDER:
                    if kind == "S" and jb[0] != "ret" and jb != ("samp", 0):
                        for w_ in waiting:
                            probs(w_)
                        waiting = [jb if jb[0] == "moba" else SAMP]
                    elif kind == "T":
                        copy_probs(jb)
                        for w_ in waiting:
                            probs(w_)
                        waiting = []
                    elif kind == "G":
                        for w_ in waiting:
                            probs(w_)
                        waiting = []
                        gate_copy(jb)

            act.wait_ge(s_gst, 1)
            gv = gmv[:].rearrange("p (h t) c -> p h t c", h=RH)
            gs = gstd[:].rearrange("p (h t) -> p h t", h=RH)
            A(gs[:, :, 0:4], gv[:, :, 0:4, 1], ACT.Sqrt, bias=C("eps"))
            A(gs[0:NS, :, 4], gv[0:NS, :, 4, 1], ACT.Sqrt, bias=C("eps", NS)).then_inc(s_gsq, 1)
            act.wait_ge(s_rst, 80)
            for t in range(TT):
                r = P if t < 4 else NS
                act.wait_ge(s_ot, 2 * t + 1)
                b = 4 + 2 * (t % 2)
                A(oT[:, 0:4, t * P:t * P + r], ps[:, b, :].rearrange("p (c n) -> p c n", c=4)[:, :, 0:r],
                  ACT.Identity).then_inc(s_otc, 1)
                if t < 4:
                    act.wait_ge(s_ot, 2 * t + 2)
                    A(oT[:, 4:8, t * P:(t + 1) * P], ps[:, b + 1, :].rearrange("p (c n) -> p c n", c=4),
                      ACT.Identity).then_inc(s_otc, 1)
                else:
                    act.wait_ge(s_ou, nO * 4 + 2)
                    A(oT[:, 4:8, NP:T], oTs[:, 4:8, :], ACT.Identity).then_inc(s_otc, 1)

            act.wait_ge(s_ghe, 2 + 16)
            A(work[:, 0:KD * T], work[:, 0:KD * T], ACT.Sigmoid).then_inc(s_gas, 1)
            for u in range(2):
                act.wait_ge(s_sto[u], 64)
            with act.Fori(0, 4) as i:
                for u in range(2):
                    act.wait_ge(s_cg, 2 * i + u + 1)
                    act.wait_ge(s_mg, 2 * i + u + 1)
                    A(gb_s[:, u].rearrange("p (h c) -> p h c", h=2), ps[:, 2 * u:2 * u + 2, 0:HALF], ACT.Sigmoid,
                      bias=bm[:, bass.ds(8 + 2 * i + u, 1)]).then_inc(s_cgs, 1)

            def std(n, r):
                act.wait_ge(s_var, n + 1)
                A(lsd[0:r, n:n + 1], lmv[0:r, n % 2, 1:2], ACT.Sqrt, bias=C("eps", r)).then_inc(s_std, 1)

            for t in range(TT):
                r = P if t < 4 else NS
                std(t, r)
                act.wait_ge(s_x1t, t + 1)
                for q in range(2):
                    m = A(x1T[:, 4 * q:4 * q + 4, t * P:t * P + r],
                          ps[:, 4 + q, :].rearrange("p (c n) -> p c n", c=4)[:, :, 0:r], ACT.Identity)
                m.then_inc(s_x1c, 1)
            act.wait_ge(s_gexp_i, 1)
            A(dgl, dgl, ACT.Exp).then_inc(s_gexp, 1)
            act.wait_ge(s_gexp_i, 2)
            A(dm, dm, ACT.Exp).then_inc(s_gexp, 1)
            act.wait_ge(s_x1s, 16 * TT)
            for t in range(TT):
                r = P if t < 4 else NS
                A(x_tm[0:r, t, :], x_tm[0:r, t, :], ACT.Identity, scale=ALPHA).then_inc(s_xa, 1)

            def copy_tokens(n, u):
                act.wait_ge(s_xt, n + 1)
                if not isinstance(n, int):
                    act.wait_ge(s_gu, n)
                for q in range(2):
                    m = A(xgT[:, u, 4 * q:4 * q + 4, :], ps[:, q, :].rearrange("p (c n) -> p c n", c=4), ACT.Identity)
                m.then_inc(s_xc, 1)

            def silu(n, u):
                act.wait_ge(s_gu, n + 2)
                g = ps[:, 2 + u, 0:4 * CAP].rearrange("p (s m n) -> p s m n", s=2, m=2)[:, :, 0, :]
                A(sg[:, u], g, ACT.Silu).then_inc(s_sl, 1)

            copy_tokens(0, 0)
            with act.Fori(0, 4) as i:
                for q in range(4):
                    n = 4 * i + q
                    act.wait_ge(s_h, n + 1)
                    silu(n, q % 2)
                    copy_tokens(n + 1, 1 - q % 2)
            act.wait_ge(s_nov, 1)
            nov = act.value_load(ev_i[0:1, 2 * OVP:2 * OVP + 1], min_val=0, max_val=OVP)
            with act.If(nov > 0):
                with act.Fori(0, nov) as i:
                    copy_tokens(PAIRS + 1 + i, 0)
                    silu(PAIRS + i, 0)
            for t in range(TT + 1):
                if t < TT:
                    std(TT + t, P if t < 4 else NS)
                if t > 0:
                    r, n = (P if t - 1 < 4 else NS), TT + t - 1
                    act.wait_ge(s_shift, t)
                    A(x_tm[0:r, t - 1, :], x_tm[0:r, t - 1, :], ACT.Identity, bias=lsh[0:r, n:n + 1],
                      scale=lsd[0:r, n:n + 1]).then_inc(s_nrm, 1)

        @block.gpsimd
        def _(pool):
            pv = nc.gpsimd
            ch = Chain(pool, pool_c)
            pool.sem_inc(s_fmc, 2)
            pool.sem_inc(s_idle, 1)
            pv.memset(zeros, 0.0).then_inc(s_zero, 1)
            with pool.Fori(0, 2) as i:
                for j in range(4):
                    n = 4 * i + j
                    pool.wait_ge(s_pev, n + 3)
                    pv.tensor_copy(fm[:, bass.ds(n, 1), :].rearrange("p o n -> p (o n)"), stage[:, j % 2]
                                   ).then_inc(s_fmc, 1)
            pool.wait_ge(s_par, 64)
            pool.wait_ge(s_sig, 1)
            for a, b, g in ((rg_t[:, 0:4, :], sig_rg[:, 0:4, :], gng.unsqueeze(1).to_broadcast([P, 4, G])),
                            (rg_t[0:NS, 4, :], sig_rg[0:NS, 4, :], gng[0:NS])):
                ch.link(pv.tensor_tensor(a, a, b, ALU.mult))
                m = pv.tensor_tensor(a, a, g, ALU.mult)
                if a.shape[0] == NS:
                    m.then_inc(s_rg, 1)
            pool.wait_ge(s_pev, 30)
            pool.wait_ge(s_trd, 22)
            pool.wait_ge(s_kst, 32)
            pool.wait_ge(s_cst, 16)
            ch.link(pv.memset(qz[:, :, :], 0.0))
            pv.tensor_tensor(qds, fm[:, 4 * FM_OF[RQ]:4 * FM_OF[RQ] + 4, NP:T],
                             C("qdec_s").rearrange("p (h q) -> p h q", h=RH), ALU.mult)
            for h in range(RH):
                m = pv.tensor_scalar(kds[:, h * P:(h + 1) * P], rk_t[0:NS, 4, h * P:(h + 1) * P],
                                     C("kdec_s", NS)[:, h:h + 1], None, ALU.mult)
            ch.link(m)
            pool.wait_ge(s_proj, 28)
            ch.link(pv.memset(logit_s[:, SLOT_AT[4]:SLOT_AT[4] + 3 * P], 0.0))
            with pool.Fori(0, 4) as i:
                def queries(u):
                    pool.wait_ge(s_s, nS * i + S_IDX[M(u, 3)] + 1)
                    pv.tensor_copy(qz[DH * u:DH * (u + 1), u, :],
                                   fm[DH * u:DH * (u + 1), bass.ds(4 * FM_OF[MQ] + i, 1), 0:NP]
                                   .rearrange("p o n -> p (o n)")).then_inc(s_stg, 1)

                queries(0)
                pool.wait_ge(s_s, nS * i + S_IDX[("ret", 3)] + 1)
                pv.tensor_copy(rk_st, fm[:, bass.ds(4 * FM_OF[RK] + i, 1), 0:NP].rearrange("p o n -> p (o n)")
                               ).then_inc(s_stg, 1)
                for u in range(2):
                    pool.wait_ge(s_s, nS * i + S_IDX[("samp", u)] + 1)
                    pool.wait_ge(s_o, nO * i + O_IDX[("skv", u)] + 1)
                    b = 2 * i + u
                    for c in range(4):
                        pv.tensor_tensor(qbd[:, u, c].rearrange("p (h q) -> p h q", h=MH),
                                         fm[:, 4 * FM_OF[MQ] + c, bass.ds(NP + SL * b, SL)]
                                         .unsqueeze(1).to_broadcast([P, MH, SL]),
                                         C("headmask").rearrange("p (c h) -> p c h", c=4)[:, c]
                                         .unsqueeze(2).to_broadcast([P, MH, SL]), ALU.mult)
                    pv.tensor_tensor(qm[:, u], qds,
                                     C("bcol").rearrange("p (b q) -> p b q", b=SB)[:, bass.ds(b, 1), :]
                                     .to_broadcast([P, RH, NS]), ALU.mult)
                    pv.tensor_tensor(km[:, u], kds, C("brow", NS)[:, bass.ds(b, 1)].to_broadcast([NS, G]), ALU.mult
                                     ).then_inc(s_stg, 1)
                pool.wait_ge(s_o, nO * i + O_IDX[("rets",)] + 1)
                pv.tensor_tensor(k_st, rk_t[:, 0:4, bass.ds(i * P, P)],
                                 C("kdec").rearrange("p (h t) -> p h t", h=RH)[:, bass.ds(i, 1), :]
                                 .rearrange("p o t -> p (o t)").unsqueeze(2).to_broadcast([P, 4, P]),
                                 ALU.mult).then_inc(s_stg, 1)
                pool.wait_ge(s_stg, 6 * i + 5)
                queries(1)
                pool.wait_ge(s_stg, 6 * i + 6)
            pool.wait_ge(s_x1s, 16 * TT)
            pool.wait_ge(s_idx, 1)
            for n in range(PAIRS + 1):
                if n >= 2:
                    pool.wait_ge(s_xt, n - 1)
                pv.indirect_dma_start(xg[:, n % 2], None, x1_d,
                                      bass.IndirectOffsetOnAxis(idx_i[:, n:n + 1].bitcast(U32), 0)
                                      ).then_inc(s_gx[n % 2], 16)
            pool.wait_ge(s_nov, 1)
            nov = pool.value_load(ev_i[0:1, 2 * OVP:2 * OVP + 1], min_val=0, max_val=OVP)
            with pool.If(nov > 0):
                with pool.Fori(0, nov) as i:
                    pool.wait_ge(s_xt, PAIRS + 1 + i)
                    pool.wait_ge(s_ovi, i + 1)
                    pool.wait_ge(s_idle, i + 1)
                    pv.tensor_tensor(idle[:], C("eps"), C("eps"), ALU.add).then_inc(s_idle, 1)
                    pv.indirect_dma_start(xg[:, 0], None, x1_d, bass.IndirectOffsetOnAxis(idx_o[:].bitcast(U32), 0)
                                          ).then_inc(s_ovg, 16)
            pool.wait_ge(s_ys[0], 16 * PAIRS // 2 + 16)
            pool.wait_ge(s_ys[1], 16 * PAIRS // 2 + 16)
            pool.wait_ge(s_ovs, nov * 16 + 16)
            pool.wait_ge(s_gu, PAIRS + nov + 1)
            pool.wait_ge(s_xc, PAIRS + 1 + nov)
            pool.wait_ge(s_idle, nov + 1)
            pv.tensor_tensor(idle[:], C("eps"), C("eps"), ALU.add)
            for t in range(TT):
                r = P if t < 4 else NS
                if t == 4:
                    pool.wait_ge(s_fru, 1)
                for c in range(2):
                    pv.indirect_dma_start(picked[0:r, t % 4, c], None, slots_d,
                                          bass.IndirectOffsetOnAxis(slot_i[0:r, c, t:t + 1].bitcast(U32), 0)
                                          ).then_inc(s_yg[t % 4], 16)
            for t in range(TT):
                r = P if t < 4 else NS
                pool.wait_ge(s_gain, t + 1)
                pv.tensor_tensor(x_tm[0:r, t, :], x_tm[0:r, t, :], ln_b[0:r], ALU.add).then_inc(s_fin, 1)

        @block.vector
        def _(dve):
            v = nc.vector
            ch = Chain(dve, dve_c)
            dve.sem_inc(s_trd, 2)
            dve.sem_inc(s_su, 2)
            dve.sem_inc(s_ou, 2)
            dve.sem_inc(s_mg, 2)
            dve.sem_inc(s_ye, 2)
            dve.sem_inc(s_cbu, 1)
            dve.sem_inc(s_h, 1)
            dve.sem_inc(s_rst, 16)
            dve.sem_inc(s_ys[0], 16)
            dve.sem_inc(s_ys[1], 16)
            dve.sem_inc(s_ovs, 16)
            with dve.Fori(0, 5) as i:
                for j in range(4):
                    n = 4 * i + j
                    dve.wait_ge(s_tr, n + 3)
                    b = 4 + 2 * (j % 2)
                    gi = tm[:, bass.ds(i, 1)].rearrange("p o t n -> p (o t) n")
                    v.tensor_copy(gi[:, 0:4, j * P:(j + 1) * P], ps[:, b, :].rearrange("p (t n) -> p t n", t=4))
                    v.tensor_copy(gi[0:NS, 4, j * P:(j + 1) * P], ps[0:NS, b + 1, 0:P]).then_inc(s_trd, 1)
            dve.wait_ge(s_cst, 16)
            dve.wait_ge(s_cross, 1)
            v.tensor_tensor(sds[0:NS], ps[0:NS, SBANK, 0:RH * NS].rearrange("p (h q) -> p h q", h=RH),
                            C("sdecay", NS).rearrange("p (h q) -> p h q", h=RH), ALU.mult).then_inc(s_ret, 1)
            dve.wait_ge(s_kst, 32)
            dve.wait_ge(s_rg, 1)
            with dve.Fori(0, 4) as i:
                def scores(jb):
                    k = S_IDX[jb]
                    bank = s_bank(jb)
                    dve.wait_ge(s_s, nS * i + nS + k + 1)
                    if jb[0] == "ret":
                        kb = jb[1]
                        w = NP - kb * P
                        if kb == 0:
                            dve.wait_ge(s_o, nO * i + O_IDX[("reto",)] + 1)
                        v.tensor_tensor(sd[:, KT_OFF[kb]:KT_OFF[kb] + w], ps[:, bank, 0:w],
                                        C("decay").rearrange("p (h n) -> p h n", h=RH)[:, bass.ds(i, 1), 0:w]
                                        .rearrange("p o n -> p (o n)"), ALU.mult).then_inc(s_su, 1)
                        return
                    if jb[0] == "moba":
                        _, u, qb = jb
                        dve.wait_ge(s_t, before_in_slot(i, jb, T_IDX, nT))
                        r, w = P, P * (qb + 1)
                        l = logit(jb, w)
                        m = v.scalar_tensor_tensor(l, C("dist")[:, 512 - w:512], C("slopes")[:, bass.ds(2 * i + u, 1)],
                                                   ps[:, bank, 0:w], ALU.mult, ALU.add)
                    else:
                        dve.wait_ge(s_t, before_in_slot(i, SAMP, T_IDX, nT))
                        r, w = 2 * NS, PAST + NS
                        rows = slice(NS * jb[1], NS * (jb[1] + 1))
                        l = logit(SAMP, w, r)
                        v.tensor_tensor(l[rows, 0:PAST], ps[rows, bank, 0:PAST], C("pastbias", r)[rows], ALU.add)
                        m = v.tensor_tensor(l[rows, PAST:w], ps[rows, bank, PAST:w],
                                            C("newbias", r)[rows, bass.ds(i * NS, NS)], ALU.add)
                    m.then_inc(s_su, 1)
                    if jb == ("samp", 0):
                        return
                    dve.wait_ge(s_su, nS * i + k + 3)
                    s_ = slot(jb)
                    v.tensor_reduce(nmax[0:r, s_:s_ + 1], l, AX, ALU.max, negate=True).then_inc(s_max, 1)

                def invert(jb, r):
                    dve.wait_ge(s_exp, nT * i + T_IDX[jb] + 1)
                    sl_ = ssum[0:r, slot(jb):slot(jb) + 1]
                    v.reciprocal(sl_, sl_).then_inc(s_inv, 1)
                    dve.wait_ge(s_inv, nT * i + INV_IDX[jb] + 1)

                def normalise():
                    invert(SAMP, 2 * NS)
                    l = logit(SAMP, PAST + NS, 2 * NS)
                    v.tensor_scalar(l, l, ssum[0:2 * NS, 4:5], None, ALU.mult).then_inc(s_pn, 1)

                def products(jb):
                    k = O_IDX[jb]
                    bank = o_bank(jb)
                    if jb[0] == "reto":
                        dve.wait_ge(s_stg, 6 * i + 5)
                    if jb[0] == "rets":
                        dve.wait_ge(s_rst, 16 * i + 16)
                    if jb[0] == "moba":
                        invert(jb, P)
                    dve.wait_ge(s_o, nO * i + nO + k + 1)
                    if jb[0] == "moba":
                        _, u, qb = jb
                        m = v.tensor_scalar(om[:, qb, bass.ds((2 * i + u) * DH, DH)], ps[:, bank, 0:DH],
                                            ssum[:, qb:qb + 1], None, ALU.mult)
                    elif jb[0] == "samp":
                        b = 2 * i + jb[1]
                        o = ps[:, bank, 0:32].rearrange("p (c h q) -> p c h q", c=4, h=2)
                        for h in range(2):
                            m = v.tensor_copy(oTs[DH * h:DH * (h + 1), 4:8, bass.ds(SL * b, SL)],
                                              o[DH * h:DH * (h + 1), :, h, :])
                    elif jb[0] == "skv":
                        for h in range(RH):
                            st = st_b[:, jb[1], h, :]
                            m = v.scalar_tensor_tensor(st, st, float(GAMMAS[h] ** SL), ps[:, bank, h * P:(h + 1) * P],
                                                       ALU.mult, ALU.add)
                    elif jb[0] == "reto":
                        v.tensor_copy(rk_t[:, 0:4, bass.ds(i * P, P)], ps[:, bank, :].rearrange("p (t n) -> p t n", t=4))
                        for qb in range(4):
                            m = v.bn_stats(gstat[:, bass.ds(i * TT + qb, 1), :].rearrange("p o c -> p (o c)"),
                                           ps[:, bank, qb * P:(qb + 1) * P])
                    else:
                        m = v.tensor_copy(rst, ps[:, bank, 0:P])
                    m.then_inc(s_ou, 1)

                for kind, jb in ORDER:
                    if kind == "S":
                        scores(jb)
                    elif kind == "N":
                        normalise()
                    elif kind == "O":
                        products(jb)

            dve.wait_ge(s_cross, 1 + SB)
            v.tensor_copy(rk_t[0:NS, 4, :], ps[0:NS, XBANK, :])
            for h in range(RH):
                m = v.bn_stats(gstat[0:NS, h * TT + 4, :], ps[0:NS, XBANK, h * P:(h + 1) * P])
            ch.link(m)
            for h in range(RH):
                for t in range(TT):
                    r = P if t < 4 else NS
                    m = v.bn_aggr(gmv[0:r, h * TT + t, :], gstat[0:r, h * TT + t, :])
            m.then_inc(s_gst, 1)
            dve.wait_ge(s_gsq, 1)
            gs = gstd[:].rearrange("p (h t) -> p h t", h=RH)
            v.reciprocal(gs[:, :, 0:4], gs[:, :, 0:4])
            ch.link(v.reciprocal(gs[0:NS, :, 4], gs[0:NS, :, 4]))
            for t in range(TT):
                r = P if t < 4 else NS
                for h in range(RH):
                    o = rk_t[0:r, t, h * P:(h + 1) * P]
                    n = h * TT + t
                    m = v.tensor_scalar(o, o, gmv[0:r, n, 0:1], gstd[0:r, n:n + 1], ALU.subtract, ALU.mult)
                ch.link(m)
                v.tensor_tensor(rg_t[0:r, t, :], rg_t[0:r, t, :], rk_t[0:r, t, :], ALU.mult).then_inc(s_gn, 1)

            dve.wait_ge(s_gas, 1)
            with dve.Fori(0, 4) as i:
                for u in range(2):
                    dve.wait_ge(s_cgs, 2 * i + u + 3)
                    dve.wait_ge(s_cb, 2 * i + u + 1)
                    mg = merged[:, bass.ds(2 * i + u, 1), :].rearrange("p o (h c) -> p (o h) c", h=2)
                    tb = t_b[:, u].rearrange("p (h c) -> p h c", h=2)
                    v.tensor_tensor(mg, mg, ps[:, 4:6, 0:HALF], ALU.mult)
                    v.tensor_tensor(tb, gb_s[:, u].rearrange("p (h c) -> p h c", h=2), ps[:, 6:8, 0:HALF], ALU.mult
                                    ).then_inc(s_cbu, 1)
                    dve.wait_ge(s_cbu, 2 * i + u + 2)
                    v.tensor_tensor(mg, mg, tb, ALU.add).then_inc(s_mg, 1)

            def row_stats(n, z, r):
                for q in range(2):
                    m = v.bn_stats(lst[0:r, n % 2, q, :], z[:, q * 512:(q + 1) * 512])
                ch.link(m)
                v.bn_aggr(lmv[0:r, n % 2], lst[0:r, n % 2].rearrange("p a b -> p (a b)")).then_inc(s_var, 1)

            def inverse_std(n, r):
                dve.wait_ge(s_std, n + 1)
                ch.link(v.reciprocal(lsd[0:r, n:n + 1], lsd[0:r, n:n + 1]))

            dve.wait_ge(s_x, 32)
            dve.wait_ge(s_ln1, 32)
            for t in range(TT):
                r = P if t < 4 else NS
                z = x_tm[0:r, t, :]
                dve.wait_ge(s_y, t + 1)
                for q in range(2):
                    m = v.scalar_tensor_tensor(z[:, q * 512:(q + 1) * 512], z[:, q * 512:(q + 1) * 512], ALPHA,
                                               ps[0:r, 2 * (t % 2) + q, :], ALU.mult, ALU.add)
                m.then_inc(s_yu, 1)
                dve.wait_ge(s_yu, t + 1)
                row_stats(t, z, r)
                inverse_std(t, r)
                ch.link(v.tensor_scalar(z, z, lmv[0:r, t % 2, 0:1], lsd[0:r, t:t + 1], ALU.subtract, ALU.mult))
                ch.link(v.tensor_tensor(z, z, ln_g[0:r], ALU.mult))
                v.tensor_tensor(z, z, ln_b[0:r], ALU.add).then_inc(s_x1, 1)

            L = ch.link
            tt_, ts_, tr_ = v.tensor_tensor, v.tensor_scalar, v.tensor_reduce

            def tmp(o, *shape):
                n = int(np.prod(shape))
                a = rtr[:, o:o + n]
                if len(shape) == 2:
                    a = a.rearrange("p (a b) -> p a b", a=shape[0])
                elif len(shape) == 3:
                    a = a.rearrange("p (a b c) -> p a b c", a=shape[0], b=shape[1])
                return a

            sel = tmp(0, TT, NE)
            s1, s2 = tmp(160, TT, NG, EPG), tmp(320, TT, NG, EPG)
            es4 = tmp(480, TT, NG, EPG)
            pos, ge = tmp(640, TT, NE), tmp(800, TT, NE)
            e5 = [tmp(960 + 40 * k, TT, EPG) for k in range(5)]
            g5 = [tmp(1160 + 20 * k, TT, NG) for k in range(4)]
            f5 = [tmp(1300 + 5 * k, TT) for k in range(12)]
            c32 = [tmp(1400 + 32 * k, NE) for k in range(5)]
            ev = tmp(1600, OVT, NE)
            evs = tmp(2260, 64)
            L(v.memset(logs, 0.0))
            dve.wait_ge(s_lg, TT)
            dve.wait_ge(s_par, 64)
            lp = ps[:, 6, 0:TT * 36].rearrange("p (t n) -> p t n", t=TT)
            tt_(logs[:, 0:4], lp[:, 0:4], br[:].unsqueeze(1).to_broadcast([P, 4, 36]), ALU.add)
            L(tt_(logs[0:NS, 4], lp[0:NS, 4], br[0:NS], ALU.add))

            def bc(a, n):
                return a.unsqueeze(2).to_broadcast([P, TT, n])

            def first_max(src, ramp, n, peak, eq, low, onehot):
                L(tr_(peak, src, AX, ALU.max))
                L(tt_(eq, src, bc(peak, n), ALU.is_ge))
                L(v.scalar_tensor_tensor(eq, eq, -64.0, C(ramp).unsqueeze(1).to_broadcast([P, TT, n]),
                                         ALU.mult, ALU.add))
                L(tr_(low, eq, AX, ALU.min))
                L(tt_(onehot, eq, bc(low, n), ALU.is_equal))

            gl = logs[:, :, 0:NG]
            el = logs[:, :, NG:NG + NE].rearrange("p t (g e) -> p t g e", g=NG)
            gmax, m1, m2, low, gsum, w1, slf = f5[0:7]
            first_max(gl, "i4", NG, gmax, g5[0], low, g5[1])
            tt_(dgl, gl, bc(gmax, NG), ALU.subtract).then_inc(s_gexp_i, 1)
            L(tt_(g5[2], g5[1], bc(C("valid"), NG), ALU.mult))
            L(tt_(es4, el, g5[1].unsqueeze(3).to_broadcast([P, TT, NG, EPG]), ALU.mult))
            es, es2, oh1, oh2, eq8 = e5
            L(tr_(es, es4.rearrange("p t g e -> p t e g"), AX, ALU.add))
            first_max(es, "i8", EPG, m1, eq8, low, oh1)
            L(v.scalar_tensor_tensor(es2, oh1, -BIG, es, ALU.mult, ALU.add))
            first_max(es2, "i8", EPG, m2, eq8, low, oh2)
            tt_(dm, m2, m1, ALU.subtract).then_inc(s_gexp_i, 1)
            for s_, oh in ((s1, oh1), (s2, oh2)):
                m = tt_(s_, oh.unsqueeze(2).to_broadcast([P, TT, NG, EPG]),
                        g5[2].unsqueeze(3).to_broadcast([P, TT, NG, EPG]), ALU.mult)
            L(m)
            flat = "p t g e -> p t (g e)"
            tt_(sel, s1.rearrange(flat), s2.rearrange(flat), ALU.add).then_inc(s_msk, 1)
            dve.wait_ge(s_gexp, 1)
            L(tr_(gsum, dgl, AX, ALU.add))
            dve.wait_ge(s_gexp, 2)
            L(ts_(w1, dm, 1.0, None, ALU.add))
            L(tt_(w1, w1, gsum, ALU.mult))
            L(v.reciprocal(wts[:, 0, :], w1))
            L(tt_(wts[:, 1, :], wts[:, 0, :], dm, ALU.mult))
            dve.wait_ge(s_pre, 1)
            tot, nov_, incl, off, one = c32
            rank = ps[:, 7, 0:TT * NE].rearrange("p (t e) -> p t e", t=TT)
            v.tensor_copy(tot, ps[:, 7, TT * NE:(TT + 1) * NE])
            v.memset(one, 1.0)
            L(v.tensor_copy(pos, rank))
            L(ts_(nov_, tot, float(CAP), None, ALU.is_gt))
            for k in range(2, T // CAP + 1):
                L(v.scalar_tensor_tensor(nov_, tot, float(CAP * k), nov_, ALU.is_gt, ALU.add))
            L(v.tensor_tensor_scan(incl, one, nov_, 0.0, ALU.mult, ALU.add))
            L(tt_(off, incl, nov_, ALU.subtract))
            L(ts_(off, off, float(CAP), float(CAP * (NE - 1)), ALU.mult, ALU.add))
            L(tt_(off, off, C("e64"), ALU.subtract))
            b32 = [P, TT, NE]
            L(ts_(ge, pos, float(CAP), None, ALU.is_ge))
            L(tt_(ge, ge, off.unsqueeze(1).to_broadcast(b32), ALU.mult))
            L(tt_(pos, pos, C("e64").unsqueeze(1).to_broadcast(b32), ALU.add))
            L(tt_(pos, pos, ge, ALU.add))
            for c, s_ in enumerate((s1, s2)):
                L(tt_(ge, pos, s_.rearrange(flat), ALU.mult))
                L(tr_(slf, ge, AX, ALU.add))
                L(v.tensor_copy(slot_i[:, c, :], slf))
            lo_i, hi_i = lohi[:, 0], lohi[:, 1]
            L(ts_(lo_i, slot_i[:], P - 1, None, ALU.bitwise_and))
            L(ts_(hi_i, slot_i[:], 7, None, ALU.logical_shift_right))
            lof, hif = tmp(2230, 2, TT), tmp(2240, 2, TT)
            v.tensor_copy(lof, lo_i)
            L(v.tensor_copy(hif, hi_i))
            for c in range(2):
                o = slice(c * TT, (c + 1) * TT)
                v.tensor_tensor(oh_lo[:, o], C("iota").unsqueeze(1).to_broadcast([P, TT, P]),
                                lof[:, c].unsqueeze(2).to_broadcast([P, TT, P]), ALU.is_equal)
                L(v.tensor_tensor(oh_hi[:, o], C("iota")[:, 0:COLS].unsqueeze(1).to_broadcast([P, TT, COLS]),
                                  hif[:, c].unsqueeze(2).to_broadcast([P, TT, COLS]), ALU.is_equal))
                v.tensor_tensor(oh_hi[:, o], oh_hi[:, o], C("tokid").unsqueeze(2).to_broadcast([P, TT, COLS]),
                                ALU.mult).then_inc(s_oh, 1)
            dve.wait_ge(s_ohu, 1)
            v.tensor_copy(idx_i[:], ps[:, 6, 256:256 + COLS]).then_inc(s_idx, 1)
            i1 = incl[0:1]
            L(tt_(ev[0:1], i1.unsqueeze(1).to_broadcast([1, OVT, NE]),
                  C("iv", 1).unsqueeze(2).to_broadcast([1, OVT, NE]), ALU.is_le))
            L(tr_(evs[0:1, 0:OVT], ev[0:1], AX, ALU.add))
            L(v.memset(ev_i[:], 0))
            L(ts_(ev_i[0:1, 0:OVT], evs[0:1, 0:OVT], float(NE - 1), None, ALU.min))
            L(ts_(evs[0:1, 32:32 + OVP], C("iota", 1)[:, 0:OVP], 2.0, incl[0:1, NE - 1:NE], ALU.mult, ALU.is_lt))
            L(tr_(evs[0:1, 50:51], evs[0:1, 32:32 + OVP], AX, ALU.add))
            v.tensor_copy(ev_i[0:1, 2 * OVP:2 * OVP + 1], evs[0:1, 50:51]).then_inc(s_nov, 1)

            def hidden(n, u):
                dve.wait_ge(s_sl, n + 1)
                up = ps[:, 2 + u, 0:4 * CAP].rearrange("p (s m n) -> p s m n", s=2, m=2)[:, :, 1, :]
                v.tensor_tensor(hid[:, u], sg[:, u], up, ALU.mult).then_inc(s_h, 1)

            def expert_rows(n, u, free):
                dve.wait_ge(s_dn, n + 1)
                free()
                for q in range(2):
                    m = v.tensor_copy(yo[:, u, q * 512:(q + 1) * 512], ps[:, 4 + 2 * u + q, :])
                m.then_inc(s_ye, 1)

            with dve.Fori(0, 4) as i:
                for q in range(4):
                    n, u = 4 * i + q, q % 2
                    hidden(n, u)
                    expert_rows(n, u, lambda: dve.wait_ge(s_ys[u], 16 * (2 * i + q // 2 + 1)))
            dve.wait_ge(s_nov, 1)
            nov = dve.value_load(ev_i[0:1, 2 * OVP:2 * OVP + 1], min_val=0, max_val=OVP)
            with dve.If(nov > 0):
                with dve.Fori(0, nov) as i:
                    v.tensor_copy(idx_o[:], idx_i[:, bass.ds(PAIRS + i, 1)]).then_inc(s_ovi, 1)
                    hidden(PAIRS + i, 0)

                    def free():
                        dve.wait_ge(s_ys[0], 16 * PAIRS // 2 + 16)
                        dve.wait_ge(s_ovs, 16 * i + 16)
                    expert_rows(PAIRS + i, 0, free)

            def weigh(t):
                r = P if t < 4 else NS
                z = x_tm[0:r, t, :]
                dve.wait_ge(s_xa, t + 1)
                dve.wait_ge(s_yg[t % 4], 32 * (t // 4 + 1))
                for c in range(2):
                    m = v.scalar_tensor_tensor(z, picked[0:r, t % 4, c], wts[0:r, c, t:t + 1], z, ALU.mult, ALU.add)
                    if c == 0:
                        L(m)
                m.then_inc(s_fru, 1)
                dve.wait_ge(s_fru, t + 1)
                row_stats(TT + t, z, r)

            def shift(t):
                r, n = (P if t < 4 else NS), TT + t
                inverse_std(n, r)
                v.scalar_tensor_tensor(lsh[0:r, n:n + 1], lmv[0:r, n % 2, 0:1], -1.0,
                                       lsd[0:r, n:n + 1], ALU.mult, ALU.mult).then_inc(s_shift, 1)

            def gain(t):
                r = P if t < 4 else NS
                dve.wait_ge(s_nrm, t + 1)
                v.tensor_tensor(x_tm[0:r, t, :], x_tm[0:r, t, :], ln_g[0:r], ALU.mult).then_inc(s_gain, 1)

            dve.wait_ge(s_ln2, 32)
            for t in range(TT):
                weigh(t)
                if t > 0:
                    shift(t - 1)
                if t > 1:
                    gain(t - 2)
            shift(TT - 1)
            gain(TT - 2)
            gain(TT - 1)


def kernel(x_prompt, x_sample, cache_k, cache_v, state_ret, page_table, w_in, b_merge, gn_g, w_br_ret, w_br_moba,
           w_out, ln1_g, ln1_b, w_router_group, b_router_group, w_router_expert, b_router_expert, w_exp_gate,
           w_exp_up, w_exp_down, ln2_g, ln2_b):
    import concourse.bacc as bacc
    from concourse.bass_utils import run_bass_kernel_spmd

    def c(a):
        return np.ascontiguousarray(a)

    def tiles(w):
        k, n = w.shape
        return w.reshape(k // P, P, n // P, P).transpose(2, 1, 0, 3).reshape(n // P, P, k)

    x = np.concatenate([np.asarray(x_prompt).reshape(NP, D), np.asarray(x_sample).reshape(NS, D)], 0)
    w = np.asarray(w_in)[0]
    at = dict(zip((RQ, RK, RV, RG, MQ, MK, MV), range(0, 7 * G, G)))
    order = [w[:, at[g]:at[g] + G] for g in (MK, RK, RV, RG, MV, MQ, RQ)] + [w[:, 7 * G:7 * G + D]]
    first = tiles(np.concatenate(order, 1))
    second = tiles(w[:, 7 * G + D:])
    branch = np.concatenate([tiles(np.asarray(w_br_ret)[0]), tiles(np.asarray(w_br_moba)[0])], 2)
    both = np.stack([second, branch], 1).reshape(2 * KD, P, D)
    wg_ = np.asarray(w_exp_gate)[0].reshape(NE, KD, P, P).transpose(0, 2, 1, 3).reshape(NE, P, D)
    wu_ = np.asarray(w_exp_up)[0].reshape(NE, KD, P, P).transpose(0, 2, 1, 3).reshape(NE, P, D)
    ck = np.asarray(cache_k)[0]
    n_pool = ck.shape[0]
    wrt = np.concatenate([np.asarray(w_router_group)[0],
                          np.asarray(w_router_expert)[0].transpose(1, 0, 2).reshape(D, NE)], 1)
    arrays = {
        "xT": c(x.T.reshape(KD, P, T).transpose(1, 0, 2)),
        "x": c(x),
        "w_tiles": c(np.concatenate([first, both], 0)),
        "w_out": c(np.asarray(w_out)[0]),
        "w_router": c(wrt.reshape(KD, P, NG + NE).transpose(1, 0, 2)),
        "b_router": c(np.concatenate([np.asarray(b_router_group)[0], np.asarray(b_router_expert)[0].reshape(NE)])),
        "b_merge": c(np.asarray(b_merge)[0].reshape(2 * KD, P).T),
        "gn_g": c(np.asarray(gn_g)[0]),
        "ln1_g": c(np.asarray(ln1_g)[0]), "ln1_b": c(np.asarray(ln1_b)[0]),
        "ln2_g": c(np.asarray(ln2_g)[0]), "ln2_b": c(np.asarray(ln2_b)[0]),
        "experts": c(np.concatenate([wg_, wu_, np.asarray(w_exp_down)[0]], 2)),
        "kT_pool": c(ck.reshape(n_pool, PAGE, 4, P).transpose(0, 2, 3, 1)),
        "v_pool": c(np.asarray(cache_v)[0].reshape(n_pool, PAGE, G)),
        "page_table": c(np.asarray(page_table).reshape(1, SB * NPG)),
        "state": c(np.asarray(state_ret)),
        "constants": constants(),
    }
    outs = [(1, NP, D), (SB, SL, D), (1, 1, NP, MH, DH), (1, 1, NP, MH, DH), (1, 1, RH, P, P),
            (1, SB, SL, MH, DH), (1, SB, SL, MH, DH), (1, SB, RH, P, P)]
    nc = bacc.Bacc("TRN2", target_bir_lowering=False, num_devices=1)
    args = [nc.dram_tensor(n, a.shape, mybir.dt.from_np(a.dtype), kind="ExternalInput").ap()
            for n, a in arrays.items()]
    args += [nc.dram_tensor(f"out_{n}", s, F32, kind="ExternalOutput").ap() for n, s in enumerate(outs)]
    args.append(nc.dram_tensor("x1_rows", (T, D), F32, kind="Internal").ap())
    args.append(nc.dram_tensor("slot_rows", (COLS * P, D), F32, kind="Internal").ap())
    hybrid_step(nc, *args)
    r = run_bass_kernel_spmd(nc, [arrays], core_ids=[0])
    return tuple(r.results[0][f"out_{n}"] for n in range(len(outs)))
```

```python
from contextlib import ExitStack

import numpy as np

import concourse.bass as bass
from concourse import mybir

F32 = mybir.dt.float32
F32R = mybir.dt.float32r
I32 = mybir.dt.int32
U32 = mybir.dt.uint32
ALU = mybir.AluOpType
ACT = mybir.ActivationFunctionType
AX = mybir.AxisListType.X

P = 128
D = 1024
KD = D // P
NP, NS = 512, 32
T = NP + NS
HALF = T // 2
TT = NP // P + 1
SB, SL = 8, 4
PAST, PAGE = 256, 128
NPG = PAST // PAGE
RH, MH, DH = 4, 8, 64
G = 512
NE, NG, EPG = 32, 4, 8
CAP = 64
PAIRS = NE // 2
OVT = (2 * T) // CAP + 1
OVP = (OVT + 1) // 2
COLS = PAIRS + OVP
ALPHA = 2.0 ** 0.25
EPS = 1e-5
BIG = 1e30
GAMMAS = [1.0 - 2.0 ** (-5.0 - h) for h in range(RH)]

MK, RK, RV, RG, MV, MQ, RQ = range(7)
FM_OF = {MK: 0, RK: 1, MQ: 2, RQ: 3}

_CW = [("ident", P), ("before", P), ("ones", P), ("iota", P), ("dist", 512), ("slopes", MH),
       ("decay", RH * 512), ("kdec", RH * 4), ("sdecay", RH * NS), ("qdec_s", RH * NS), ("kdec_s", RH),
       ("bcol", SB * NS), ("brow", SB), ("headmask", 4 * MH), ("pastbias", PAST), ("newbias", SB // 2 * NS),
       ("i4", NG), ("i8", EPG), ("e64", NE), ("tokid", TT), ("valid", TT), ("iv", OVT), ("eps", 1)]
CO = {}
_o = 0
for _n, _w in _CW:
    CO[_n] = (_o, _w)
    _o += _w
NCONST = _o


def constants():
    c = np.zeros((P, NCONST), np.float64)

    def put(name, rows, val):
        o, w = CO[name]
        c[:rows, o:o + w] = np.asarray(val, np.float64).reshape(rows, w)

    p = np.arange(P)
    put("ident", P, np.eye(P))
    put("before", P, (p[:, None] < p[None, :]))
    put("ones", P, np.ones((P, P)))
    put("iota", P, np.tile(p, (P, 1)))
    d = np.arange(512)[None, :] - 384 - p[:, None]
    put("dist", P, np.where(d <= 0, d, -BIG))
    slopes = 2.0 ** (-8.0 * np.arange(1, MH + 1) / MH)
    put("slopes", P, np.tile(slopes, (P, 1)))
    lg = np.log(np.array(GAMMAS))
    ks = float(P) ** -0.5
    m = np.arange(512)[None, :] - p[:, None]
    put("decay", P, np.stack([np.where(m >= 0, ks * np.exp(g * np.maximum(m, 0)), 0) for g in lg], 1))
    put("kdec", P, np.stack([ks * np.exp(g * (NP - 1 - (np.arange(4)[None, :] * P + p[:, None]))) for g in lg], 1))
    j = np.arange(NS)
    same = (j[:, None] // SL == j[None, :] // SL)
    dt = (j[None, :] - j[:, None])
    put("sdecay", NS, np.stack([np.where(same & (dt >= 0), ks * np.exp(g * np.maximum(dt, 0)), 0) for g in lg], 1))
    put("qdec_s", P, np.tile(np.stack([np.exp(g * (j % SL + 1)) for g in lg], 0)[None], (P, 1, 1)))
    put("kdec_s", NS, np.stack([ks * np.exp(g * (SL - 1 - j % SL)) for g in lg], 1))
    put("bcol", P, np.tile((np.arange(SB)[:, None] == j[None, :] // SL)[None], (P, 1, 1)))
    put("brow", NS, (j[:, None] // SL == np.arange(SB)[None, :]))
    hp = np.arange(4)[None, :, None] * 2 + (p[:, None, None] // DH)
    put("headmask", P, (hp == np.arange(MH)[None, None, :]))
    q = np.arange(MH * SL)
    put("pastbias", 2 * MH * SL, np.tile(slopes[q // SL][:, None] * (np.arange(PAST)[None, :] - (PAST + q % SL)[:, None]),
                                        (2, 1)))
    nb = np.full((2, MH * SL, SB // 2, NS), -BIG)
    for b in range(SB):
        for k in range(SL):
            ok = q % SL >= k
            nb[b % 2, ok, b // 2, SL * b + k] = (slopes[q // SL] * (k - q % SL))[ok]
    put("newbias", 2 * MH * SL, nb)
    put("i4", P, np.tile(np.arange(NG), (P, 1)))
    put("i8", P, np.tile(np.arange(EPG), (P, 1)))
    put("e64", P, np.tile(CAP * np.arange(NE), (P, 1)))
    tok = p[:, None] + P * np.arange(TT)[None, :]
    put("tokid", P, np.where(tok < T, tok, 0))
    put("valid", P, tok < T)
    put("iv", P, np.tile(np.arange(OVT), (P, 1)))
    put("eps", P, np.full((P, 1), EPS))
    return c.astype(np.float32)


class Chain:

    def __init__(self, eng, sem):
        self.eng, self.sem, self.n = eng, sem, 0

    def mark(self, ins):
        ins.then_inc(self.sem, 1)
        self.n += 1
        return self.n

    def wait(self, value):
        self.eng.wait_ge(self.sem, value)

    def link(self, ins):
        self.wait(self.mark(ins))


def hybrid_step(nc, xT_d, x_d, w_tiles, w_out_d, w_router, b_router, b_merge, gn_g, ln1_g, ln1_b, ln2_g, ln2_b,
                experts_d, kT_pool, v_pool, page_table, state_d, const_d,
                y_prompt, y_sample, k_prompt, v_prompt, ret_prompt, k_sample, v_sample, ret_sample,
                x1_d, slots_d):
    with ExitStack() as ctx:
        def sb(name, shape, dt=F32):
            return ctx.enter_context(nc.sbuf_tensor(name, shape, dt))

        def sem(name):
            return ctx.enter_context(nc.semaphore(name))

        OM, TM = 0, 2560
        XT = TM + 5 * 2560
        FM = XT + KD * T
        RING = 5120
        EW = 3 * D
        ARENA = RING + 8 * EW
        WO = RING
        assert FM + 16 * T <= ARENA and WO + 8 * D <= RING + 3 * EW

        def under(pad, tensors):
            with ExitStack() as here:
                if pad:
                    here.enter_context(nc.sbuf_tensor(f"pad_{tensors[0][0]}", [P, pad], F32))
                return [here.enter_context(nc.sbuf_tensor(n, shape, F32R)) for n, shape in tensors]

        w_hi1, w_lo1 = under(0, [("w_hi1", [P, D]), ("w_lo1", [P, D])])
        o_lo, = under(XT, [("o_lo", [P, KD, T])])
        xc_hi, xc_lo = under(FM, [("xc_hi", [P, KD, T]), ("xc_lo", [P, KD, T])])
        arena = sb("arena", [P, ARENA])

        def tile3(base, a, b, rows=P):
            return arena[0:rows, base:base + a * b].rearrange("p (a b) -> p a b", a=a)

        om = tile3(OM, TT, G)
        tm = arena[:, TM:TM + 5 * 2560].rearrange("p (g t n) -> p g t n", g=5, t=TT)
        xT = tile3(XT, KD, T)
        fm = tile3(FM, 16, T)
        rk_t, rv_t, rg_t, mv_t = (tm[:, g] for g in (RK, RV, RG, MV))
        wo = tile3(WO, KD, D)
        x_tm = tile3(0, TT, D)

        def expert(s):
            if s >= 8:
                return (cst[:, P:P + EW], scratch[:, 2048:2048 + EW],
                        w_ring[:, :, :].rearrange("p a n -> p (a n)")[:, 0:EW])[s - 8]
            at = RING + (s + 3) % 8 * EW
            return arena[:, at:at + EW]

        xa_hi, xa_lo = under(0, [("xa_hi", [P, KD, T]), ("xa_lo", [P, KD, T])])
        o_hi, = under(KD * T, [("o_hi", [P, KD, T])])
        work = sb("work", [P, 2 * KD * T])
        merged = work[:, 0:KD * T].rearrange("p (k t) -> p k t", k=KD)
        kv_s = work[:, 4352:8448].rearrange("p (u m n) -> p u m n", u=2, m=2)
        x1T = work[:, 4352:8704].rearrange("p (k t) -> p k t", k=KD)
        rst = work[:, 8448:8576]
        xg = work[:, 0:2048].rearrange("p (u n) -> p u n", u=2)
        xgT = work[:, 2048:4096].rearrange("p (u k t) -> p u k t", u=2, k=KD)
        yo = work[:, 4352:6400].rearrange("p (u n) -> p u n", u=2)
        sg = work[:, 6400:6656].rearrange("p (u n) -> p u n", u=2)
        hid = work[:, 6656:6912].rearrange("p (u n) -> p u n", u=2)
        hidT = work[:, 6912:7168].rearrange("p (u n) -> p u n", u=2)
        picked = work[:, 0:8192].rearrange("p (u c n) -> p u c n", u=4, c=2)

        w_ring = sb("w_ring", [P, 4, D])
        cst = sb("cst", [P, NCONST])
        wr = sb("wr", [P, KD, NG + NE])
        br = sb("br", [P, NG + NE])
        bm = sb("bm", [P, 16])
        w_hi0, w_lo0 = under(3072, [("w_hi0", [P, D]), ("w_lo0", [P, D])])
        w_hi, w_lo = [w_hi0, w_hi1], [w_lo0, w_lo1]
        scratch = sb("scratch", [P, 5120])
        small = sb("small", [P, 2, 5])
        st_b = scratch[:, 0:1024].rearrange("p (u h v) -> p u h v", u=2, h=RH)
        rk_st = scratch[:, 1024:1536]
        k_st = scratch[:, 1536:2048].rearrange("p (t d) -> p t d", t=4)
        qz = scratch[:, 2048:3072].rearrange("p (u n) -> p u n", u=2)
        sd = scratch[:, 3072:4352]
        qbd = scratch[:, 4352:4608].rearrange("p (u c q) -> p u c q", u=2, c=4)
        qm = scratch[:, 4608:4864].rearrange("p (u h q) -> p u h q", u=2, h=RH)
        qds = scratch[:, 4864:4992].rearrange("p (h q) -> p h q", h=RH)
        sds = scratch[:, 4992:5120].rearrange("p (h q) -> p h q", h=RH)
        km = tile3(TM, 2, G, NS)
        SLOT_AT = [0, P, 3 * P, 6 * P, 10 * P]
        logit_s = w_ring[:, 2:4, :].rearrange("p a n -> p (a n)")
        pt_s = arena[:, TM + 1024:TM + 2560]
        spare = FM + 16 * T
        kds = arena[0:NS, spare + 512:spare + 1024]
        oTs = tile3(spare + 1024, KD, NS)
        zeros = scratch[:, 2048:3072]
        gng = arena[:, 2048:2048 + G]
        stage = scratch[:, 0:1088].rearrange("p (u t) -> p u t", u=2)
        gb_s = scratch[:, 0:1088].rearrange("p (u t) -> p u t", u=2)
        t_b = scratch[:, 1088:2176].rearrange("p (u t) -> p u t", u=2)
        ln_g = scratch[:, 0:1024]
        ln_b = scratch[:, 1024:2048]
        logs = scratch[:, 2048:2048 + TT * 36].rearrange("p (t n) -> p t n", t=TT)
        rtr = scratch[:, 2304:5120]

        oh_lo = work[:, 0:2 * TT * P].rearrange("p (n q) -> p n q", n=2 * TT)
        oh_hi = work[:, 2 * TT * P:2 * TT * (P + COLS)].rearrange("p (n q) -> p n q", n=2 * TT)
        nmax, ssum = small[:, 0], small[:, 1]
        gstat = sb("gstat", [P, RH * TT, 6])
        gmv = sb("gmv", [P, RH * TT, 2])
        gstd = sb("gstd", [P, RH * TT])
        lst = sb("lst", [P, 2, 2, 6])
        lmv = sb("lmv", [P, 2, 2])
        lsd = sb("lsd", [P, 2 * TT])
        lsh = sb("lsh", [P, 2 * TT])
        wts = sb("wts", [P, 2, TT])
        slot_i = sb("slot_i", [P, 2, TT], I32)
        idx_i = sb("idx_i", [P, COLS], I32)
        idx_o = sb("idx_o", [P, 1], I32)
        ev_i = sb("ev_i", [1, 2 * OVP + 2], I32)
        pt_i = sb("pt_i", [1, SB * NPG], I32)

        ps = ctx.enter_context(nc.psum_tensor("ps", [P, 8, 512], F32))

        def C(name, rows=P):
            o, w = CO[name]
            return cst[0:rows, o:o + w]

        ident = C("ident")

        XQ = 4
        s_xT = [sem(f"xT_loaded{q}") for q in range(XQ)]
        s_id = sem("identity_loaded")
        s_w = [sem(f"w_tile_loaded{j}") for j in range(4)]
        s_par = sem("parameters_loaded")
        s_cst = sem("constants_loaded")
        s_pt = sem("page_table_loaded")
        s_kv = [sem(f"pages_loaded{u}") for u in range(2)]
        s_idle = sem("idle_written")
        s_zero = sem("zeros_made")
        s_z = sem("overflow_rows_cleared")
        s_rst = sem("head_state_stored")
        s_st = [sem(f"state_loaded{u}") for u in range(2)]
        s_sto = [sem(f"state_stored{u}") for u in range(2)]
        s_proj = sem("proj_done")
        s_pev = sem("proj_evacuated")
        s_tr = sem("group_transposed")
        s_trd = sem("token_major_written")
        s_fmc = sem("feature_major_copied")
        s_kst = sem("k_stored")
        s_out = sem("outputs_stored")
        s_hi = sem("weights_high_parts")
        s_xs = sem("x_piece_split")
        s_sp = sem("weights_split")
        s_xch = sem("x_high_parts")
        s_xcl = sem("x_low_parts")
        s_olo = sem("branch_low_parts")
        s_gsp = sem("second_gate_weights_split")
        s_bsp = sem("branch_weights_split")
        s_sig = sem("rg_silu")
        s_rg = sem("rg_gated")
        dve_c = sem("dve_chain")
        pool_c = sem("pool_chain")
        s_gh = sem("gate_half_done")
        s_ghe = sem("gate_half_evacuated")
        s_s = sem("scores_ready")
        s_su = sem("scores_used")
        s_max = sem("logits_ready")
        s_exp = sem("exp_done")
        s_inv = sem("sums_inverted")
        s_pn = sem("sample_probs_ready")
        s_t = sem("probs_transposed")
        s_tu = sem("probs_copied")
        s_o = sem("products_ready")
        s_ou = sem("products_used")
        s_stg = sem("staged")
        s_ret = sem("retention_state_ready")
        s_cross = sem("sample_retention_ready")
        s_gst = sem("group_stats_ready")
        s_gsq = sem("group_std_ready")
        s_gn = sem("branch_rows_ready")
        s_ot = sem("branch_transposed")
        s_otc = sem("branch_copied")
        s_gas = sem("first_gate_ready")
        s_cg = sem("second_gate_projected")
        s_cgs = sem("second_gate_ready")
        s_cb = sem("branches_done")
        s_cbu = sem("branches_used")
        s_mg = sem("merged_ready")
        s_wo = sem("w_out_loaded")
        s_x = sem("x_loaded")
        s_ln1 = sem("ln1_loaded")
        s_ln2 = sem("ln2_loaded")
        s_y = sem("y_done")
        s_yu = sem("y_used")
        s_var = sem("variance_ready")
        s_std = sem("std_ready")
        s_x1 = sem("x1_ready")
        s_x1s = sem("x1_stored")
        s_x1t = sem("x1_transposed")
        s_x1c = sem("x1_copied")
        s_lg = sem("router_logits_ready")
        s_gexp_i = sem("router_exp_in")
        s_gexp = sem("router_exp_done")
        s_msk = sem("selection_ready")
        s_pre = sem("ranks_ready")
        s_oh = sem("slot_onehots_ready")
        s_ohu = sem("slot_onehots_used")
        s_idx = sem("slot_tokens_ready")
        s_nov = sem("overflow_count_ready")
        s_e = [sem(f"expert_loaded{s}") for s in range(8)]
        s_last = [sem(f"last_experts_loaded{s}") for s in range(3)]
        s_gx = [sem(f"tokens_gathered{u}") for u in range(2)]
        s_xt = sem("tokens_transposed")
        s_xc = sem("tokens_copied")
        s_gu = sem("gate_up_done")
        s_sl = sem("silu_done")
        s_h = sem("hidden_ready")
        s_ht = sem("hidden_transposed")
        s_hc = sem("hidden_copied")
        s_dn = sem("down_done")
        s_ye = sem("expert_rows_evacuated")
        s_ys = [sem(f"expert_rows_stored{u}") for u in range(2)]
        s_ovi = sem("overflow_index_ready")
        s_ovg = sem("overflow_gathered")
        s_ovw = sem("overflow_weights")
        s_ovs = sem("overflow_stored")
        s_yg = [sem(f"rows_gathered{u}") for u in range(4)]
        s_xa = sem("x1_scaled")
        s_shift = sem("row_shift_ready")
        s_nrm = sem("rows_normalised")
        s_gain = sem("rows_scaled")
        s_fin = sem("final_ready")
        s_finl = sem("final_sample_ready")
        s_fru = sem("rows_used")

        block = ctx.enter_context(nc.Block())

        idle = sb("idle", [P, 1])
        dgl = sb("dgl", [P, TT, NG])[:]
        dm = sb("dm", [P, TT])[:]
        lohi = sb("lohi", [P, 2, 2, TT], I32)

        def M(u, qb):
            return ("moba", u, qb)

        SAMP = ("samp",)
        ORDER = [("S", M(0, 0)), ("S", M(0, 1)), ("G", 0),
                 ("S", M(0, 2)), ("T", M(0, 0)), ("S", ("ret", 0)), ("O", M(0, 0)),
                 ("S", M(0, 3)), ("T", M(0, 1)), ("S", ("ret", 1)), ("O", M(0, 1)),
                 ("S", ("samp", 0)), ("T", M(0, 2)), ("S", ("samp", 1)), ("O", M(0, 2)), ("S", ("ret", 2)),
                 ("O", ("skv", 0)),
                 ("S", M(1, 0)), ("T", M(0, 3)), ("S", ("ret", 3)), ("O", M(0, 3)), ("G", 1),
                 ("S", M(1, 1)), ("N", SAMP), ("T", SAMP), ("O", ("skv", 1)), ("O", ("samp", 0)), ("O", ("samp", 1)),
                 ("S", M(1, 2)), ("T", M(1, 0)), ("O", ("reto",)), ("O", M(1, 0)),
                 ("S", M(1, 3)), ("T", M(1, 1)), ("O", ("rets",)), ("O", M(1, 1)),
                 ("G", 2), ("T", M(1, 2)), ("G", 3), ("T", M(1, 3)), ("O", M(1, 2)), ("O", M(1, 3))]
        KT_OFF = [0, 512, 896, 1152]

        def places(kind):
            return {jb: n for n, jb in enumerate([jb for k, jb in ORDER if k == kind])}

        S_IDX, T_IDX, O_IDX = places("S"), places("T"), places("O")
        nS, nT, nO = len(S_IDX), len(T_IDX), len(O_IDX)
        INV_IDX = {jb: n for n, jb in enumerate([jb for k, jb in ORDER if k == "N" or k == "O" and jb[0] == "moba"])}
        assert nS % 2 == 0 and nO % 2 == 0

        def slot(jb):
            return jb[2] if jb[0] == "moba" else 4

        def before_in_slot(i, jb, idx, n):
            if jb[0] == "moba" and jb[1] == 1:
                return n * i + n + idx[M(0, jb[2])] + 1
            return n * i + idx[M(1, jb[2]) if jb[0] == "moba" else jb] + 1

        def logit(jb, w, rows=P):
            return logit_s[0:rows, SLOT_AT[slot(jb)]:SLOT_AT[slot(jb)] + w]

        def pt(jb, w):
            return pt_s[:, SLOT_AT[slot(jb)]:SLOT_AT[slot(jb)] + w]

        SBANK, TBANK, OBANK, XBANK = 2, 4, 5, 7

        def s_bank(jb):
            return SBANK + S_IDX[jb] % 2

        def o_bank(jb):
            return OBANK + O_IDX[jb] % 2

        def wgu(s, k):
            return expert(s)[:, 2 * k * P:2 * (k + 1) * P]

        def pair_slots(i, q):
            if isinstance(i, int) and i == 3 and q >= 2:
                return [(4, 8), (9, 10)][q - 2]
            return 2 * q, 2 * q + 1

        def wd(s, half):
            return expert(s)[:, 2 * D + half * 512:2 * D + (half + 1) * 512]

        @block.sync
        def _(sp):
            def w_tile(n):
                return w_tiles[bass.ds(n, 1)] if not isinstance(n, int) else w_tiles[n]

            for j in range(4):
                if j == 1:
                    sp.wait_ge(s_xT[XQ - 2], 16)
                sp.dma_start(w_ring[:, j, :], w_tile(j)).then_inc(s_w[j], 16)
            sp.dma_start(cst[:, P:NCONST], const_d[:, P:NCONST]).then_inc(s_cst, 16)
            with sp.Fori(1, 7) as i:
                for j in range(4):
                    sp.wait_ge(s_sp, 4 * i + j - 3)
                    sp.dma_start(w_ring[:, j, :], w_tile(4 * i + j)).then_inc(s_w[j], 16)
            kp = k_prompt.rearrange("d b (t p) h e -> p (d b t) (h e)", p=P)
            vp = v_prompt.rearrange("d b (t p) h e -> p (d b t) (h e)", p=P)
            ks_ = k_sample.rearrange("d b l h e -> (d b l) (h e)")
            vs_ = v_sample.rearrange("d b l h e -> (d b l) (h e)")
            sp.wait_ge(s_trd, 2 + 4)
            sp.dma_start(kp, tm[:, MK, 0:4, :]).then_inc(s_kst, 16)
            sp.dma_start(ks_, tm[0:NS, MK, 4, :]).then_inc(s_kst, 16)
            sp.wait_ge(s_trd, 2 + 20)
            sp.dma_start(vp, tm[:, MV, 0:4, :]).then_inc(s_out, 16)
            sp.dma_start(vs_, tm[0:NS, MV, 4, :]).then_inc(s_out, 16)
            stv = state_d.rearrange("d b h k v -> k (d b) h v")
            sto = ret_sample.rearrange("d b h k v -> k (d b) h v")

            def pages(b, u):
                for pg in range(NPG):
                    r = sp.value_load(pt_i[0:1, bass.ds(b * NPG + pg, 1)], min_val=0, max_val=kT_pool.shape[0] - 1)
                    sp.dma_start(kv_s[:, u, 0, :].rearrange("p (c t) -> p c t", c=4)[:, :, pg * PAGE:(pg + 1) * PAGE],
                                 kT_pool[bass.ds(r, 1)].rearrange("o c p t -> p (o c) t")).then_inc(s_kv[u], 16)
                    sp.dma_start(kv_s[:, u, 1, pg * 512:(pg + 1) * 512],
                                 v_pool[bass.ds(r, 1)].rearrange("o p n -> p (o n)")).then_inc(s_kv[u], 16)

            sp.wait_ge(s_pt, 16)
            for u in range(2):
                sp.wait_ge(s_sp, 25 + u)
                sp.dma_start(w_ring[:, u, :], w_tile(28 + u)).then_inc(s_w[u], 16)
            sp.wait_ge(s_proj, 28)
            for u in range(2):
                pages(u, u)
            sp.wait_ge(s_fmc, 10)
            sp.wait_ge(s_tr, 2 + 20)
            for u in range(2):
                sp.dma_start(st_b[:, u], stv[:, u]).then_inc(s_st[u], 16)
            rpv = ret_prompt.rearrange("d b h k v -> (d b h) k v")

            def store_pass(i, refill):
                for u in range(2):
                    sp.wait_ge(s_ou, nO * i + 2 + O_IDX[("skv", u)] + 1)
                    sp.dma_start(sto[:, bass.ds(2 * i + u, 1)].rearrange("k o h v -> k (o h) v"),
                                 st_b[:, u]).then_inc(s_sto[u], 16)
                if refill:
                    sp.wait_ge(s_gh, 4 * i + 2)
                    sp.dma_start(w_ring[:, 0, :], w_tile(30 + 2 * i)).then_inc(s_w[0], 16)
                    for u in range(2):
                        sp.wait_ge(s_sto[u], 16 * (i + 1))
                        sp.dma_start(st_b[:, u], stv[:, bass.ds(2 * i + 2 + u, 1)].rearrange("k o h v -> k (o h) v")
                                     ).then_inc(s_st[u], 16)
                        sp.wait_ge(s_o, nO * i + nO + O_IDX[("samp", u)] + 1)
                        pages(2 * i + 2 + u, u)
                sp.wait_ge(s_ou, nO * i + 2 + O_IDX[("rets",)] + 1)
                sp.dma_start(rpv[bass.ds(i, 1)].rearrange("o k v -> (o k) v"), rst).then_inc(s_rst, 16)
                if refill:
                    sp.wait_ge(s_gh, 4 * i + 4)
                    sp.dma_start(w_ring[:, 1, :], w_tile(31 + 2 * i)).then_inc(s_w[1], 16)

            with sp.Fori(0, 3) as i:
                store_pass(i, True)
            store_pass(3, False)
            for u in range(2):
                sp.wait_ge(s_gh, 14 + 2 * u)
                sp.dma_start(w_ring[:, u, :], w_tile(36 + u)).then_inc(s_w[u], 16)
            sp.wait_ge(s_t, 5 * nT)
            for u in range(2):
                sp.dma_start(w_ring[:, 2 + u, :], w_tile(38 + u)).then_inc(s_w[2 + u], 16)
            wov = w_out_d.rearrange("(k p) n -> p k n", p=P)
            for n in range(2, KD):
                if n < 4:
                    sp.wait_ge(s_cg, n - 1)
                else:
                    sp.wait_ge(s_gsp, n - 3)
                sp.dma_start(w_ring[:, 2 * (n % 2), :], w_tile(36 + 2 * n)).then_inc(s_w[2 * (n % 2)], 16)
                sp.wait_ge(s_bsp, n - 1)
                sp.dma_start(w_ring[:, 2 * (n % 2) + 1, :], w_tile(37 + 2 * n)).then_inc(s_w[2 * (n % 2) + 1], 16)
                if n == 3:
                    sp.wait_ge(s_otc, 2 * TT)
                if 3 <= n < 7:
                    sp.dma_start(wo[:, 2 * n - 6:2 * n - 4], wov[:, 2 * n - 6:2 * n - 4]).then_inc(s_wo, 16)
            sp.wait_ge(s_cg, 8)
            sp.dma_start(x_tm[:, 0:4, :], x_d[0:NP].rearrange("(t p) n -> p t n", p=P)).then_inc(s_x, 16)
            sp.dma_start(x_tm[0:NS, 4, :], x_d[NP:T]).then_inc(s_x, 16)
            sp.wait_ge(s_cb, 8)
            sp.wait_ge(s_mg, 10)
            sp.dma_start(ln_g, ln1_g.partition_broadcast(P)).then_inc(s_ln1, 16)
            sp.dma_start(ln_b, ln1_b.partition_broadcast(P)).then_inc(s_ln1, 16)
            for s in range(5):
                sp.dma_start(expert(s), experts_d[s]).then_inc(s_e[s], 16)
            sp.dma_start(expert(10), experts_d[NE - 1]).then_inc(s_last[2], 16)
            for t in range(TT):
                sp.wait_ge(s_x1, t + 1)
                rows = P if t < 4 else NS
                sp.dma_start(x1_d[t * P:t * P + rows], x_tm[0:rows, t, :]).then_inc(s_x1s, 16)
            sp.wait_ge(s_y, TT)
            for s in (5, 6, 7):
                sp.dma_start(expert(s), experts_d[s]).then_inc(s_e[s], 16)
            sp.dma_start(ln_g, ln2_g.partition_broadcast(P)).then_inc(s_ln2, 16)
            sp.dma_start(ln_b, ln2_b.partition_broadcast(P)).then_inc(s_ln2, 16)
            yv = slots_d.rearrange("(c p) n -> c p n", p=P)

            def store_pair(n, u):
                sp.wait_ge(s_ye, n + 3)
                sp.dma_start(yv[bass.ds(n, 1)].rearrange("o p n -> (o p) n"), yo[:, u]).then_inc(s_ys[u], 16)

            sp.wait_ge(s_nov, 1)
            sp.wait_ge(s_idx, 1)
            for s in (0, 1):
                sp.dma_start(expert(8 + s), experts_d[NE - 3 + s]).then_inc(s_last[s], 16)
            with sp.Fori(0, 2) as i:
                for q in range(4):
                    sp.wait_ge(s_dn, 4 * i + q + 1)
                    for s in (2 * q, 2 * q + 1):
                        sp.dma_start(expert(s), experts_d[bass.ds(8 * i + 8 + s, 1)].rearrange("o p n -> (o p) n")
                                     ).then_inc(s_e[s], 16)
                    store_pair(4 * i + q, q % 2)
            for q in range(8):
                if q < 3:
                    sp.wait_ge(s_dn, 8 + q + 1)
                    for s in (2 * q, 2 * q + 1) if q < 2 else (4,):
                        sp.dma_start(expert(s), experts_d[24 + s]).then_inc(s_e[s], 16)
                store_pair(8 + q, q % 2)
            sp.wait_ge(s_nov, 1)
            nov = sp.value_load(ev_i[0:1, 2 * OVP:2 * OVP + 1], min_val=0, max_val=OVP)
            with sp.If(nov > 0):
                with sp.Fori(0, nov) as i:
                    sp.wait_ge(s_dn, PAIRS + i)
                    for s in range(2):
                        e = sp.value_load(ev_i[0:1, bass.ds(2 * i + s, 1)], min_val=0, max_val=NE - 1)
                        sp.dma_start(expert(s), experts_d[bass.ds(e, 1)].rearrange("o p n -> (o p) n")
                                     ).then_inc(s_ovw, 16)
                    sp.wait_ge(s_ye, PAIRS + i + 3)
                    sp.dma_start(yv[bass.ds(PAIRS + i, 1)].rearrange("o p n -> (o p) n"), yo[:, 0]).then_inc(s_ovs, 16)
            for t in range(4):
                sp.wait_ge(s_fin, t + 1)
                sp.dma_start(y_prompt[0, t * P:(t + 1) * P, :], x_tm[:, t, :]).then_inc(s_out, 16)
            sp.wait_ge(s_finl, 1)
            sp.dma_start(y_sample.rearrange("b l n -> (b l) n"), x_tm[0:NS, 4, :]).then_inc(s_out, 16)
            sp.wait_ge(s_sto[0], 64)
            sp.wait_ge(s_sto[1], 64)
            sp.wait_ge(s_x1s, 16 * TT)
            sp.wait_ge(s_rst, 80)
            sp.wait_ge(s_out, 16 * (2 + TT))

        @block.tensor
        def _(pe):
            mm = nc.tensor.matmul

            def tr(out, in_, rows):
                return nc.tensor.transpose(out, in_, ident[0:rows, 0:rows])

            def project_half(slot, bank, half):
                for k in range(KD):
                    m = mm(ps[:, bank, 0:HALF], w_ring[:, slot, k * P:(k + 1) * P],
                           xT[:, k, half * HALF:(half + 1) * HALF], start=k == 0, stop=k == KD - 1)
                return m

            def split_products(out, b, k_w, x_hi, x_lo, k_x, cols, start, stop):
                w = slice(k_w * P, (k_w + 1) * P)
                mm(out, w_hi[b][:, w], x_hi[:, k_x, cols], start=start, stop=False)
                mm(out, w_hi[b][:, w], x_lo[:, k_x, cols], start=False, stop=False)
                return mm(out, w_lo[b][:, w], x_hi[:, k_x, cols], start=False, stop=stop)

            def project_split(b, bank, half, x_hi, x_lo, first=False):
                for k in range(KD):
                    if first and k % (KD // XQ) == 0:
                        pe.wait_ge(s_xs, k // (KD // XQ) + 1)
                    m = split_products(ps[:, bank, 0:HALF], b, k, x_hi, x_lo, k,
                                       slice(half * HALF, (half + 1) * HALF), k == 0, k == KD - 1)
                return m

            pe.sem_inc(s_tr, 2)
            pe.sem_inc(s_s, nS)
            pe.sem_inc(s_t, nT)
            pe.sem_inc(s_o, nO)
            pe.sem_inc(s_gu, 1)

            def group(i, token_major):
                for j in range(4):
                    n = 4 * i + j
                    pe.wait_ge(s_sp, n + 1)
                    pe.wait_ge(s_pev, n + 1)
                    project_split(j % 2, 2 * (j % 2), 0, xa_hi, xa_lo, first=j == 0 and token_major)
                    project_split(j % 2, 2 * (j % 2) + 1, 1, xa_hi, xa_lo).then_inc(s_proj, 1)
                    if token_major:
                        if j > 0:
                            turn(n - 1, j - 1)
                if token_major:
                    turn(4 * i + 3, 3)

            def turn(n, j):
                pe.wait_ge(s_pev, n + 3)
                pe.wait_ge(s_trd, n + 1)
                pe.wait_ge(s_id, 16)
                b = 4 + 2 * (j % 2)
                for t in range(4):
                    tr(ps[:, b, t * P:(t + 1) * P], stage[:, j % 2, t * P:(t + 1) * P], P)
                tr(ps[0:NS, b + 1, 0:P], stage[:, j % 2, NP:T], P).then_inc(s_tr, 1)

            with pe.Fori(0, 5) as i:
                group(i, True)
            with pe.Fori(5, 7) as i:
                group(i, False)

            pe.wait_ge(s_pev, 30)
            pe.wait_ge(s_trd, 22)
            for h in range(RH):
                m = mm(ps[0:NS, SBANK, h * NS:(h + 1) * NS], fm[:, 4 * FM_OF[RK] + h, NP:T],
                       fm[:, 4 * FM_OF[RQ] + h, NP:T], start=True, stop=True)
            m.then_inc(s_cross, 1)
            pe.wait_ge(s_ret, 1)
            for h in range(RH):
                mm(ps[0:NS, XBANK, h * P:(h + 1) * P], sds[0:NS, h, :], rv_t[0:NS, 4, h * P:(h + 1) * P],
                   start=h == 0, stop=False, skip_group_check=True)

            def gate_half(i, q):
                u, half = q // 2, q % 2
                if half == 0:
                    pe.wait_ge(s_w[u], 16 * (7 + i + 1))
                pe.wait_ge(s_ghe, 4 * i + q + 1)
                project_half(u, q % 2, half).then_inc(s_gh, 1)

            with pe.Fori(0, 4) as i:
                def scores(jb):
                    k = S_IDX[jb]
                    b = s_bank(jb)
                    pe.wait_ge(s_su, nS * i + k + 1)
                    if jb[0] == "moba":
                        _, u, qb = jb
                        if qb == 0:
                            pe.wait_ge(s_stg, 6 * i + [1, 6][u])
                        m = mm(ps[:, b, 0:P * (qb + 1)], qz[:, u, qb * P:(qb + 1) * P],
                               fm[:, bass.ds(i, 1), 0:P * (qb + 1)].rearrange("p o n -> p (o n)"),
                               start=True, stop=True)
                    elif jb[0] == "ret":
                        kb = jb[1]
                        if kb == 0:
                            pe.wait_ge(s_stg, 6 * i + 2)
                        w = NP - kb * P
                        m = mm(ps[:, b, 0:w], rk_st[:, kb * P:(kb + 1) * P],
                               fm[:, bass.ds(4 * FM_OF[RQ] + i, 1), kb * P:NP].rearrange("p o n -> p (o n)"),
                               start=True, stop=True)
                    else:
                        u = jb[1]
                        pe.wait_ge(s_stg, 6 * i + 3 + u)
                        pe.wait_ge(s_kv[u], 64 * (i + 1))
                        for c in range(4):
                            mm(ps[NS * u:NS * (u + 1), b, 0:PAST], qbd[:, u, c, :], kv_s[:, u, 0, c * PAST:(c + 1) * PAST],
                               start=c == 0, stop=c == 3)
                        for c in range(4):
                            m = mm(ps[NS * u:NS * (u + 1), b, PAST:PAST + NS], qbd[:, u, c, :],
                                   fm[:, 4 * FM_OF[MK] + c, NP:T], start=c == 0, stop=c == 3)
                    m.then_inc(s_s, 1)

                def turns(jb):
                    t = T_IDX[jb]
                    if jb[0] == "moba":
                        pe.wait_ge(s_exp, nT * i + t + 1)
                    else:
                        pe.wait_ge(s_pn, i + 1)
                    pe.wait_ge(s_tu, nT * i + t + 1)
                    for kb in range(jb[2] + 1 if jb[0] == "moba" else NPG + 1):
                        m = tr(ps[:, TBANK, kb * P:(kb + 1) * P], logit(jb, 4 * P)[:, kb * P:(kb + 1) * P], P)
                    m.then_inc(s_t, 1)

                def products(jb):
                    k = O_IDX[jb]
                    b = o_bank(jb)
                    pe.wait_ge(s_ou, nO * i + k + 1)
                    if jb[0] in ("moba", "samp"):
                        tj = jb if jb[0] == "moba" else SAMP
                        pe.wait_ge(s_tu, nT * i + T_IDX[tj] + 2)
                    if jb[0] == "moba":
                        _, u, qb = jb
                        for kb in range(qb + 1):
                            m = mm(ps[:, b, 0:DH], pt(jb, 4 * P)[:, kb * P:(kb + 1) * P],
                                   mv_t[:, kb, bass.ds((2 * i + u) * DH, DH)], start=kb == 0, stop=kb == qb)
                    elif jb[0] == "samp":
                        u = jb[1]
                        pr = pt(SAMP, 3 * 2 * NS).rearrange("p (k q) -> p k q", k=3)[:, :, u * NS:(u + 1) * NS]
                        for c in range(4):
                            for src in range(NPG + 1):
                                for h in range(2):
                                    cols = slice(c * P + h * DH, c * P + (h + 1) * DH)
                                    q = slice(8 * c + SL * h, 8 * c + SL * (h + 1))
                                    o = ps[h * DH:(h + 1) * DH, b, q]
                                    if src < NPG:
                                        m = mm(o, kv_s[:, u, 1, src * G:(src + 1) * G][:, cols], pr[:, src, q],
                                               start=src == 0, stop=False)
                                    else:
                                        m = mm(o, mv_t[0:NS, 4, cols], pr[0:NS, NPG, q], start=False, stop=True)
                    elif jb[0] == "skv":
                        u = jb[1]
                        for h in range(RH):
                            if h == 0:
                                pe.wait_ge(s_st[u], 16 * (i + 1))
                            x = mm(ps[0:NS, XBANK, h * P:(h + 1) * P], qm[:, u, h, :], st_b[:, u, h, :],
                                   start=False, stop=False, skip_group_check=True)
                        x.then_inc(s_cross, 1)
                        for h in range(RH):
                            m = mm(ps[:, b, h * P:(h + 1) * P], km[0:NS, u, h * P:(h + 1) * P],
                                   rv_t[0:NS, 4, h * P:(h + 1) * P], start=True, stop=True)
                    elif jb[0] == "reto":
                        pe.wait_ge(s_su, nS * i + 2 + S_IDX[("ret", 3)] + 1)
                        for qb in range(4):
                            for kb in range(qb + 1):
                                o = KT_OFF[kb] + (qb - kb) * P
                                m = mm(ps[:, b, qb * P:(qb + 1) * P], sd[:, o:o + P],
                                       rv_t[:, kb, bass.ds(i * P, P)], start=kb == 0, stop=kb == qb)
                    else:
                        pe.wait_ge(s_stg, 6 * i + 5)
                        for kb in range(4):
                            m = mm(ps[:, b, 0:P], k_st[:, kb, :], rv_t[:, kb, bass.ds(i * P, P)],
                                   start=kb == 0, stop=kb == 3)
                    m.then_inc(s_o, 1)

                for kind, jb in ORDER:
                    if kind == "S":
                        scores(jb)
                    elif kind == "T":
                        turns(jb)
                    elif kind == "O":
                        products(jb)
                    elif kind == "G":
                        gate_half(i, jb)

            def second_gate(n, u):
                pe.wait_ge(s_w[2 * u], 16 * [12, 8][u])
                pe.wait_ge(s_cgs, n + 1)
                project_half(2 * u, 2 * u, 0)
                project_half(2 * u, 2 * u + 1, 1).then_inc(s_cg, 1)

            pe.wait_ge(s_ghe, 18)
            pe.wait_ge(s_su, nS * 4 + 2)
            for u in range(2):
                second_gate(u, u)
            pe.wait_ge(s_tu, 4 * nT + 1)
            pe.wait_ge(s_ou, nO * 4 + 2)
            for t in range(TT):
                r = P if t < 4 else NS
                pe.wait_ge(s_gn, t + 1)
                if t >= 2:
                    pe.wait_ge(s_olo, 2 * t - 3)
                b = 4 + 2 * (t % 2)
                for c in range(4):
                    m = tr(ps[:, b, c * P:c * P + r], rg_t[0:r, t, c * P:(c + 1) * P], r)
                m.then_inc(s_ot, 1)
                if t < 4:
                    if t >= 2:
                        pe.wait_ge(s_olo, 2 * t - 2)
                    for c in range(4):
                        m = tr(ps[:, b + 1, c * P:(c + 1) * P], om[:, t, c * P:(c + 1) * P], P)
                    m.then_inc(s_ot, 1)
            pe.wait_ge(s_olo, 2 * TT)
            pe.wait_ge(s_xcl, 1)

            def branches(n):
                pe.wait_ge(s_bsp, n + 1)
                pe.wait_ge(s_cbu, n + 1)
                for br_ in range(2):
                    for half in range(2):
                        for k in range(4):
                            kk = 4 * br_ + k
                            m = split_products(ps[:, 4 + 2 * br_ + half, 0:HALF], 0, kk, o_hi, o_lo, kk,
                                               slice(half * HALF, (half + 1) * HALF), k == 0, k == 3)
                m.then_inc(s_cb, 1)

            with pe.Fori(0, 3) as i:
                for u in range(2):
                    n = 2 * i + u
                    branches(n)
                    pe.wait_ge(s_gsp, n + 1)
                    pe.wait_ge(s_cgs, n + 3)
                    project_split(1, 2 * u, 0, xc_hi, xc_lo)
                    project_split(1, 2 * u + 1, 1, xc_hi, xc_lo).then_inc(s_cg, 1)
            for n in (6, 7):
                branches(n)

            def turn_x1(t):
                r = P if t < 4 else NS
                pe.wait_ge(s_x1, t + 1)
                pe.wait_ge(s_x1c, t)
                for k in range(KD):
                    m = tr(ps[:, 4 + k // 4, (k % 4) * P:(k % 4) * P + r], x_tm[0:r, t, k * P:(k + 1) * P], r)
                m.then_inc(s_x1t, 1)

            def router(t):
                r = P if t < 4 else NS
                pe.wait_ge(s_x1c, t + 1)
                for k in range(KD):
                    m = mm(ps[0:r, 6, t * 36:(t + 1) * 36], x1T[:, k, t * P:t * P + r], wr[:, k, :],
                           start=k == 0, stop=k == KD - 1)
                m.then_inc(s_lg, 1)

            pe.wait_ge(s_wo, 64)
            pe.wait_ge(s_mg, 10)
            pe.wait_ge(s_cgs, 10)
            for t in range(TT):
                r = P if t < 4 else NS
                if t >= 2:
                    pe.wait_ge(s_yu, t - 1)
                for half in range(2):
                    for k in range(KD):
                        m = mm(ps[0:r, 2 * (t % 2) + half, :], merged[:, k, t * P:t * P + r],
                               wo[:, k, half * 512:(half + 1) * 512], start=k == 0, stop=k == KD - 1)
                    if half == 0 and t > 1:
                        router(t - 2)
                m.then_inc(s_y, 1)
                if t > 0:
                    turn_x1(t - 1)
            router(TT - 2)
            turn_x1(TT - 1)
            router(TT - 1)
            pe.wait_ge(s_cbu, 9)
            pe.wait_ge(s_msk, 1)
            sel = rtr[:, 0:TT * NE].rearrange("p (t e) -> p t e", t=TT)
            rank_of = ps[:, 7, 0:(TT + 1) * NE].rearrange("p (t e) -> p t e", t=TT + 1)
            mm(rank_of[:, 0], C("before"), sel[:, 0], start=True, stop=True)
            for s in range(TT):
                mm(rank_of[:, s + 1:TT + 1], C("ones"), sel[:, s:s + 1].to_broadcast([P, TT - s, NE]),
                   start=s == 0, stop=False, skip_group_check=True)
            mm(rank_of[:, 1:TT], C("before"), sel[:, 1:TT], start=False, stop=True, skip_group_check=True
               ).then_inc(s_pre, 1)
            for n in range(2 * TT):
                if n % TT == 0:
                    pe.wait_ge(s_oh, n // TT + 1)
                m = mm(ps[:, 6, 256:256 + COLS], oh_lo[:, n], oh_hi[:, n], start=n == 0, stop=n == 2 * TT - 1)
            m.then_inc(s_ohu, 1)

            def turn_tokens(n, u, par):
                pe.wait_ge(s_gx[u], par)
                pe.wait_ge(s_xc, n)
                for k in range(KD):
                    m = tr(ps[:, k // 4, (k % 4) * P:(k % 4 + 1) * P], xg[:, u, k * P:(k + 1) * P], P)
                m.then_inc(s_xt, 1)

            def gate_up(slots, u, loaded):
                for s in range(2):
                    pe.wait_ge(*loaded(slots[s]))
                for k in range(KD):
                    for s in range(2):
                        m = mm(ps[s * CAP:(s + 1) * CAP, 2 + u, 0:2 * P], xgT[:, u, k, s * CAP:(s + 1) * CAP],
                               wgu(slots[s], k), start=k == 0, stop=k == KD - 1)
                m.then_inc(s_gu, 1)

            def turn_hidden(n, u):
                pe.wait_ge(s_h, n + 2)
                tr(ps[:, 2 + u, 2 * P:3 * P], hid[:, u], P).then_inc(s_ht, 1)

            def down(n, slots, u):
                pe.wait_ge(s_hc, n + 1)
                pe.wait_ge(s_ye, n + 1)
                for half in range(2):
                    for s in range(2):
                        m = mm(ps[s * CAP:(s + 1) * CAP, 4 + 2 * u + half, :], hidT[:, u, s * CAP:(s + 1) * CAP],
                               wd(slots[s], half), start=True, stop=True)
                m.then_inc(s_dn, 1)

            pe.wait_ge(s_x1c, TT)
            pe.wait_ge(s_idx, 1)
            turn_tokens(0, 0, 16)
            def four_pairs(i):
                for q in range(4):
                    n, u = 4 * i + q, q % 2
                    pe.wait_ge(s_xc, n + 1)
                    gate_up(pair_slots(i, q), u, lambda s: (s_e[s], 16 * (i + 1)) if s < 8 else (s_last[s - 8], 16))
                    turn_tokens(n + 1, 1 - u, 16 * (2 * i + (q + 1) // 2 + 1))
                    if isinstance(n, int) and n == 0:
                        turn_hidden(n, u)
                        continue
                    down(n - 1, pair_slots(i, q - 1) if q else (6, 7), 1 - u)
                    turn_hidden(n, u)

            four_pairs(0)
            with pe.Fori(1, 3) as i:
                four_pairs(i)
            four_pairs(3)
            down(PAIRS - 1, pair_slots(3, 3), 1)
            pe.wait_ge(s_nov, 1)
            nov = pe.value_load(ev_i[0:1, 2 * OVP:2 * OVP + 1], min_val=0, max_val=OVP)
            with pe.If(nov > 0):
                with pe.Fori(0, nov) as i:
                    pe.wait_ge(s_ovg, 16 * (i + 1))
                    pe.wait_ge(s_xc, PAIRS + 1 + i)
                    for k in range(KD):
                        m = tr(ps[:, k // 4, (k % 4) * P:(k % 4 + 1) * P], xg[:, 0, k * P:(k + 1) * P], P)
                    m.then_inc(s_xt, 1)
                    pe.wait_ge(s_xc, PAIRS + 2 + i)
                    gate_up((0, 1), 0, lambda s: (s_ovw, 32 * (i + 1)))
                    turn_hidden(PAIRS + i, 0)
                    pe.wait_ge(s_ye, PAIRS + i + 2)
                    down(PAIRS + i, (0, 1), 0)

        @block.scalar
        def _(act):
            A = nc.scalar.activation
            for q in range(XQ):
                act.dma_start(xT[:, q * KD // XQ:(q + 1) * KD // XQ, :], xT_d[:, q * KD // XQ:(q + 1) * KD // XQ, :]
                              ).then_inc(s_xT[q], 16)
            act.dma_start(ident, const_d[:, 0:P]).then_inc(s_id, 16)
            act.dma_start(pt_i[:], page_table).then_inc(s_pt, 16)
            act.dma_start(bm[:], b_merge).then_inc(s_par, 16)
            act.dma_start(gng, gn_g.partition_broadcast(P)).then_inc(s_par, 16)
            act.dma_start(wr[:], w_router).then_inc(s_par, 16)
            act.dma_start(br[:], b_router.partition_broadcast(P)).then_inc(s_par, 16)
            act.sem_inc(s_pev, 2)
            act.sem_inc(s_ghe, 2)
            act.sem_inc(s_cgs, 2)
            act.sem_inc(s_tu, 1)

            def to_stage(i, copied):
                for j in range(4):
                    n = 4 * i + j
                    act.wait_ge(s_proj, n + 1)
                    act.wait_ge(s_tr, n + 1)
                    if copied:
                        act.wait_ge(s_fmc, n + 1)
                    A(stage[:, j % 2].rearrange("p (h c) -> p h c", h=2), ps[:, 2 * (j % 2):2 * (j % 2) + 2, 0:HALF],
                      ACT.Identity).then_inc(s_pev, 1)

            with act.Fori(0, 2) as i:
                to_stage(i, True)
            act.wait_ge(s_zero, 1)
            act.dma_start(slots_d.rearrange("(c p) n -> p c n", p=P)[:, PAIRS:COLS, :],
                          zeros.unsqueeze(1).to_broadcast([P, OVP, D])).then_inc(s_z, 16)
            act.wait_ge(s_fmc, 10)
            with act.Fori(2, 5) as i:
                to_stage(i, False)
            act.wait_ge(s_trd, 2 + 16)
            A(rg_t[:, 0:4, :], rg_t[:, 0:4, :], ACT.Silu)
            A(rg_t[0:NS, 4, :], rg_t[0:NS, 4, :], ACT.Silu).then_inc(s_sig, 1)
            for g in (MQ, RQ):
                for j in range(4):
                    act.wait_ge(s_proj, 4 * g + j + 1)
                    A(fm[:, 4 * FM_OF[g] + j, :].rearrange("p (h c) -> p h c", h=2),
                      ps[:, 2 * (j % 2):2 * (j % 2) + 2, 0:HALF], ACT.Identity,
                      scale=DH ** -0.5 if g == MQ else 1.0).then_inc(s_pev, 1)

            act.wait_ge(s_par, 64)
            with act.Fori(0, 4) as i:
                def gate_copy(q):
                    u, half = q // 2, q % 2
                    act.wait_ge(s_gh, 4 * i + q + 1)
                    A(merged[:, bass.ds(2 * i + u, 1), half * HALF:(half + 1) * HALF].rearrange("p o n -> p (o n)"),
                      ps[:, q % 2, 0:HALF], ACT.Identity, bias=bm[:, bass.ds(2 * i + u, 1)]).then_inc(s_ghe, 1)

                def probs(jb):
                    t = T_IDX[jb]
                    act.wait_ge(s_max, nT * i + t + 1)
                    r, w = (P, P * (jb[2] + 1)) if jb[0] == "moba" else (2 * NS, PAST + NS)
                    s_ = slot(jb)
                    A(logit(jb, w, r), logit(jb, w, r), ACT.Exp, bias=nmax[0:r, s_:s_ + 1],
                      accum_out=ssum[0:r, s_:s_ + 1]).then_inc(s_exp, 1)

                def copy_probs(jb):
                    act.wait_ge(s_t, nT * i + nT + T_IDX[jb] + 1)
                    if jb[0] == "moba":
                        act.wait_ge(s_o, before_in_slot(i, jb, O_IDX, nO))
                        w = P * (jb[2] + 1)
                        A(pt(jb, w), ps[:, TBANK, 0:w], ACT.Identity).then_inc(s_tu, 1)
                    else:
                        act.wait_ge(s_o, nO * i + O_IDX[("samp", 1)] + 1)
                        A(pt(jb, 6 * NS).rearrange("p (k q) -> p k q", k=3),
                          ps[:, TBANK, 0:3 * P].rearrange("p (k q) -> p k q", k=3)[:, :, 0:2 * NS],
                          ACT.Identity).then_inc(s_tu, 1)

                waiting = []
                for kind, jb in ORDER:
                    if kind == "S" and jb[0] != "ret" and jb != ("samp", 0):
                        for w_ in waiting:
                            probs(w_)
                        waiting = [jb if jb[0] == "moba" else SAMP]
                    elif kind == "T":
                        copy_probs(jb)
                        for w_ in waiting:
                            probs(w_)
                        waiting = []
                    elif kind == "G":
                        for w_ in waiting:
                            probs(w_)
                        waiting = []
                        gate_copy(jb)

            act.wait_ge(s_s, 5 * nS)
            A(xc_hi[:, :, :], xT, ACT.Identity).then_inc(s_xch, 1)
            act.wait_ge(s_gst, 1)
            gv = gmv[:].rearrange("p (h t) c -> p h t c", h=RH)
            gs = gstd[:].rearrange("p (h t) -> p h t", h=RH)
            A(gs[:, :, 0:4], gv[:, :, 0:4, 1], ACT.Sqrt, bias=C("eps"))
            A(gs[0:NS, :, 4], gv[0:NS, :, 4, 1], ACT.Sqrt, bias=C("eps", NS)).then_inc(s_gsq, 1)
            act.wait_ge(s_rst, 80)
            for t in range(TT):
                r = P if t < 4 else NS
                act.wait_ge(s_ot, 2 * t + 1)
                b = 4 + 2 * (t % 2)
                A(o_hi[:, 0:4, t * P:t * P + r], ps[:, b, :].rearrange("p (c n) -> p c n", c=4)[:, :, 0:r],
                  ACT.Identity).then_inc(s_otc, 1)
                if t < 4:
                    act.wait_ge(s_ot, 2 * t + 2)
                    A(o_hi[:, 4:8, t * P:(t + 1) * P], ps[:, b + 1, :].rearrange("p (c n) -> p c n", c=4),
                      ACT.Identity).then_inc(s_otc, 1)
                else:
                    act.wait_ge(s_ou, nO * 4 + 2)
                    A(o_hi[:, 4:8, NP:T], oTs[:, 4:8, :], ACT.Identity).then_inc(s_otc, 1)

            act.wait_ge(s_ghe, 2 + 16)
            A(work[:, 0:KD * T], work[:, 0:KD * T], ACT.Sigmoid).then_inc(s_gas, 1)
            for u in range(2):
                act.wait_ge(s_sto[u], 64)
            with act.Fori(0, 4) as i:
                for u in range(2):
                    act.wait_ge(s_cg, 2 * i + u + 1)
                    act.wait_ge(s_mg, 2 * i + u + 1)
                    A(gb_s[:, u].rearrange("p (h c) -> p h c", h=2), ps[:, 2 * u:2 * u + 2, 0:HALF], ACT.Sigmoid,
                      bias=bm[:, bass.ds(8 + 2 * i + u, 1)]).then_inc(s_cgs, 1)

            def std(n, r):
                act.wait_ge(s_var, n + 1)
                A(lsd[0:r, n:n + 1], lmv[0:r, n % 2, 1:2], ACT.Sqrt, bias=C("eps", r)).then_inc(s_std, 1)

            for t in range(TT):
                r = P if t < 4 else NS
                std(t, r)
                act.wait_ge(s_x1t, t + 1)
                for q in range(2):
                    m = A(x1T[:, 4 * q:4 * q + 4, t * P:t * P + r],
                          ps[:, 4 + q, :].rearrange("p (c n) -> p c n", c=4)[:, :, 0:r], ACT.Identity)
                m.then_inc(s_x1c, 1)
            act.wait_ge(s_gexp_i, 1)
            A(dgl, dgl, ACT.Exp).then_inc(s_gexp, 1)
            act.wait_ge(s_gexp_i, 2)
            A(dm, dm, ACT.Exp).then_inc(s_gexp, 1)
            act.wait_ge(s_x1s, 16 * TT)
            for t in range(TT):
                r = P if t < 4 else NS
                A(x_tm[0:r, t, :], x_tm[0:r, t, :], ACT.Identity, scale=ALPHA).then_inc(s_xa, 1)

            def copy_tokens(n, u):
                act.wait_ge(s_xt, n + 1)
                if not isinstance(n, int):
                    act.wait_ge(s_gu, n)
                for q in range(2):
                    m = A(xgT[:, u, 4 * q:4 * q + 4, :], ps[:, q, :].rearrange("p (c n) -> p c n", c=4), ACT.Identity)
                m.then_inc(s_xc, 1)

            def silu(n, u):
                act.wait_ge(s_gu, n + 2)
                A(sg[:, u], ps[:, 2 + u, 0:P], ACT.Silu).then_inc(s_sl, 1)

            def copy_hidden(n, u):
                act.wait_ge(s_ht, n + 1)
                A(hidT[:, u], ps[:, 2 + u, 2 * P:3 * P], ACT.Identity).then_inc(s_hc, 1)

            copy_tokens(0, 0)
            with act.Fori(0, 4) as i:
                for q in range(4):
                    n = 4 * i + q
                    act.wait_ge(s_h, n + 1)
                    silu(n, q % 2)
                    copy_tokens(n + 1, 1 - q % 2)
                    copy_hidden(n, q % 2)
            act.wait_ge(s_nov, 1)
            nov = act.value_load(ev_i[0:1, 2 * OVP:2 * OVP + 1], min_val=0, max_val=OVP)
            with act.If(nov > 0):
                with act.Fori(0, nov) as i:
                    copy_tokens(PAIRS + 1 + i, 0)
                    silu(PAIRS + i, 0)
                    copy_hidden(PAIRS + i, 0)
            for t in range(TT + 1):
                if t < TT:
                    std(TT + t, P if t < 4 else NS)
                if t > 0:
                    r, n = (P if t - 1 < 4 else NS), TT + t - 1
                    act.wait_ge(s_shift, t)
                    A(x_tm[0:r, t - 1, :], x_tm[0:r, t - 1, :], ACT.Identity, bias=lsh[0:r, n:n + 1],
                      scale=lsd[0:r, n:n + 1]).then_inc(s_nrm, 1)

        @block.gpsimd
        def _(pool):
            pv = nc.gpsimd
            ch = Chain(pool, pool_c)
            pool.sem_inc(s_fmc, 2)
            pool.sem_inc(s_idle, 1)
            pv.memset(zeros, 0.0).then_inc(s_zero, 1)
            with pool.Fori(0, 2) as i:
                for j in range(4):
                    n = 4 * i + j
                    pool.wait_ge(s_pev, n + 3)
                    pv.tensor_copy(fm[:, bass.ds(n, 1), :].rearrange("p o n -> p (o n)"), stage[:, j % 2]
                                   ).then_inc(s_fmc, 1)
            pool.wait_ge(s_cst, 16)
            pool.wait_ge(s_trd, 2 + 8)
            for h in range(RH):
                m = pv.tensor_scalar(kds[:, h * P:(h + 1) * P], rk_t[0:NS, 4, h * P:(h + 1) * P],
                                     C("kdec_s", NS)[:, h:h + 1], None, ALU.mult)
            pool.wait_ge(s_par, 64)
            pool.wait_ge(s_sig, 1)
            pv.tensor_tensor(rg_t[:, 0:4, :], rg_t[:, 0:4, :], gng.unsqueeze(1).to_broadcast([P, 4, G]), ALU.mult)
            pv.tensor_tensor(rg_t[0:NS, 4, :], rg_t[0:NS, 4, :], gng[0:NS], ALU.mult).then_inc(s_rg, 1)
            pool.wait_ge(s_rg, 1)
            pool.wait_ge(s_pev, 30)
            pool.wait_ge(s_trd, 22)
            pool.wait_ge(s_kst, 32)
            pv.tensor_tensor(qds, fm[:, 4 * FM_OF[RQ]:4 * FM_OF[RQ] + 4, NP:T],
                             C("qdec_s").rearrange("p (h q) -> p h q", h=RH), ALU.mult)
            pool.wait_ge(s_sp, 28)
            ch.link(pv.memset(logit_s[:, SLOT_AT[4]:SLOT_AT[4] + 3 * P], 0.0))
            pool.wait_ge(s_z, 16)
            with pool.Fori(0, 4) as i:
                def queries(u):
                    pool.wait_ge(s_s, nS * i + S_IDX[M(u, 3)] + 1)
                    pv.tensor_copy(qz[DH * u:DH * (u + 1), u, :],
                                   fm[DH * u:DH * (u + 1), bass.ds(4 * FM_OF[MQ] + i, 1), 0:NP]
                                   .rearrange("p o n -> p (o n)")).then_inc(s_stg, 1)

                queries(0)
                pool.wait_ge(s_s, nS * i + S_IDX[("ret", 3)] + 1)
                pv.tensor_copy(rk_st, fm[:, bass.ds(4 * FM_OF[RK] + i, 1), 0:NP].rearrange("p o n -> p (o n)")
                               ).then_inc(s_stg, 1)
                for u in range(2):
                    pool.wait_ge(s_s, nS * i + S_IDX[("samp", u)] + 1)
                    pool.wait_ge(s_o, nO * i + O_IDX[("skv", u)] + 1)
                    b = 2 * i + u
                    for c in range(4):
                        pv.tensor_tensor(qbd[:, u, c].rearrange("p (h q) -> p h q", h=MH),
                                         fm[:, 4 * FM_OF[MQ] + c, bass.ds(NP + SL * b, SL)]
                                         .unsqueeze(1).to_broadcast([P, MH, SL]),
                                         C("headmask").rearrange("p (c h) -> p c h", c=4)[:, c]
                                         .unsqueeze(2).to_broadcast([P, MH, SL]), ALU.mult)
                    pv.tensor_tensor(qm[:, u], qds,
                                     C("bcol").rearrange("p (b q) -> p b q", b=SB)[:, bass.ds(b, 1), :]
                                     .to_broadcast([P, RH, NS]), ALU.mult)
                    pv.tensor_tensor(km[:, u], kds, C("brow", NS)[:, bass.ds(b, 1)].to_broadcast([NS, G]), ALU.mult
                                     ).then_inc(s_stg, 1)
                pool.wait_ge(s_o, nO * i + O_IDX[("rets",)] + 1)
                pv.tensor_tensor(k_st, rk_t[:, 0:4, bass.ds(i * P, P)],
                                 C("kdec").rearrange("p (h t) -> p h t", h=RH)[:, bass.ds(i, 1), :]
                                 .rearrange("p o t -> p (o t)").unsqueeze(2).to_broadcast([P, 4, P]),
                                 ALU.mult).then_inc(s_stg, 1)
                pool.wait_ge(s_stg, 6 * i + 5)
                queries(1)
                pool.wait_ge(s_stg, 6 * i + 6)
            pool.wait_ge(s_xch, 1)
            pv.tensor_tensor(xc_lo[:, :, :], xT, xc_hi[:, :, :].bitcast(F32), ALU.subtract).then_inc(s_xcl, 1)
            pool.wait_ge(s_x1s, 16 * TT)
            pool.wait_ge(s_idx, 1)
            for n in range(PAIRS + 1):
                if n >= 2:
                    pool.wait_ge(s_xt, n - 1)
                pv.indirect_dma_start(xg[:, n % 2], None, x1_d,
                                      bass.IndirectOffsetOnAxis(idx_i[:, n:n + 1].bitcast(U32), 0)
                                      ).then_inc(s_gx[n % 2], 16)
            pool.wait_ge(s_nov, 1)
            nov = pool.value_load(ev_i[0:1, 2 * OVP:2 * OVP + 1], min_val=0, max_val=OVP)
            with pool.If(nov > 0):
                with pool.Fori(0, nov) as i:
                    pool.wait_ge(s_xt, PAIRS + 1 + i)
                    pool.wait_ge(s_ovi, i + 1)
                    pool.wait_ge(s_idle, i + 1)
                    pv.tensor_tensor(idle[:], C("eps"), C("eps"), ALU.add).then_inc(s_idle, 1)
                    pv.indirect_dma_start(xg[:, 0], None, x1_d, bass.IndirectOffsetOnAxis(idx_o[:].bitcast(U32), 0)
                                          ).then_inc(s_ovg, 16)
            pool.wait_ge(s_ys[0], 16 * PAIRS // 2 + 16)
            pool.wait_ge(s_ys[1], 16 * PAIRS // 2 + 16)
            pool.wait_ge(s_ovs, nov * 16 + 16)
            pool.wait_ge(s_gu, PAIRS + nov + 1)
            pool.wait_ge(s_xc, PAIRS + 1 + nov)
            pool.wait_ge(s_idle, nov + 1)
            pv.tensor_tensor(idle[:], C("eps"), C("eps"), ALU.add)
            for t in range(TT):
                r = P if t < 4 else NS
                if t == 4:
                    pool.wait_ge(s_fru, 1)
                for c in range(2):
                    pv.indirect_dma_start(picked[0:r, t % 4, c], None, slots_d,
                                          bass.IndirectOffsetOnAxis(slot_i[0:r, c, t:t + 1].bitcast(U32), 0)
                                          ).then_inc(s_yg[t % 4], 16)
            for t in range(TT - 1):
                pool.wait_ge(s_gain, t + 1)
                pv.tensor_tensor(x_tm[:, t, :], x_tm[:, t, :], ln_b, ALU.add).then_inc(s_fin, 1)

        @block.vector
        def _(dve):
            v = nc.vector
            ch = Chain(dve, dve_c)
            dve.sem_inc(s_trd, 2)
            dve.sem_inc(s_su, 2)
            dve.sem_inc(s_ou, 2)
            dve.sem_inc(s_mg, 2)
            dve.sem_inc(s_ye, 2)
            dve.sem_inc(s_cbu, 1)
            dve.sem_inc(s_h, 1)
            dve.sem_inc(s_rst, 16)
            dve.sem_inc(s_ys[0], 16)
            dve.sem_inc(s_ys[1], 16)
            dve.sem_inc(s_ovs, 16)
            def split_weights(b, j, loaded, split_before, done):
                dve.wait_ge(s_w[j], loaded)
                v.tensor_copy(w_hi[b][:], w_ring[:, j, :]).then_inc(s_hi, 1)
                dve.wait_ge(s_hi, split_before + 1)
                v.tensor_tensor(w_lo[b][:], w_ring[:, j, :], w_hi[b][:].bitcast(F32), ALU.subtract).then_inc(done, 1)

            split_weights(0, 0, 16, 0, s_sp)
            for q in range(XQ):
                k = slice(q * KD // XQ, (q + 1) * KD // XQ)
                dve.wait_ge(s_xT[q], 16)
                ch.link(v.tensor_copy(xa_hi[:, k, :], xT[:, k, :]))
                v.tensor_tensor(xa_lo[:, k, :], xT[:, k, :], xa_hi[:, k, :].bitcast(F32), ALU.subtract
                                ).then_inc(s_xs, 1)
            split_weights(1, 1, 16, 1, s_sp)
            with dve.Fori(0, 5) as i:
                for j in range(4):
                    n = 4 * i + j
                    dve.wait_ge(s_proj, n + 1)
                    split_weights(j % 2, (j + 2) % 4, 16 * (i + (j + 2) // 4 + 1), n + 2, s_sp)
                    dve.wait_ge(s_tr, n + 3)
                    b = 4 + 2 * (j % 2)
                    gi = tm[:, bass.ds(i, 1)].rearrange("p o t n -> p (o t) n")
                    v.tensor_copy(gi[:, 0:4, j * P:(j + 1) * P], ps[:, b, :].rearrange("p (t n) -> p t n", t=4))
                    v.tensor_copy(gi[0:NS, 4, j * P:(j + 1) * P], ps[0:NS, b + 1, 0:P]).then_inc(s_trd, 1)
            for n in range(20, 26):
                dve.wait_ge(s_proj, n + 1)
                split_weights(n % 2, (n + 2) % 4, 16 * ((n + 2) // 4 + 1), n + 2, s_sp)
            dve.wait_ge(s_cst, 16)
            dve.wait_ge(s_cross, 1)
            v.tensor_tensor(sds[0:NS], ps[0:NS, SBANK, 0:RH * NS].rearrange("p (h q) -> p h q", h=RH),
                            C("sdecay", NS).rearrange("p (h q) -> p h q", h=RH), ALU.mult).then_inc(s_ret, 1)
            dve.wait_ge(s_kst, 32)
            dve.wait_ge(s_rg, 1)
            with dve.Fori(0, 4) as i:
                def scores(jb):
                    k = S_IDX[jb]
                    bank = s_bank(jb)
                    dve.wait_ge(s_s, nS * i + nS + k + 1)
                    if jb[0] == "ret":
                        kb = jb[1]
                        w = NP - kb * P
                        if kb == 0:
                            dve.wait_ge(s_o, nO * i + O_IDX[("reto",)] + 1)
                        v.tensor_tensor(sd[:, KT_OFF[kb]:KT_OFF[kb] + w], ps[:, bank, 0:w],
                                        C("decay").rearrange("p (h n) -> p h n", h=RH)[:, bass.ds(i, 1), 0:w]
                                        .rearrange("p o n -> p (o n)"), ALU.mult).then_inc(s_su, 1)
                        return
                    if jb[0] == "moba":
                        _, u, qb = jb
                        dve.wait_ge(s_t, before_in_slot(i, jb, T_IDX, nT))
                        r, w = P, P * (qb + 1)
                        l = logit(jb, w)
                        m = v.scalar_tensor_tensor(l, C("dist")[:, 512 - w:512], C("slopes")[:, bass.ds(2 * i + u, 1)],
                                                   ps[:, bank, 0:w], ALU.mult, ALU.add)
                    else:
                        dve.wait_ge(s_t, before_in_slot(i, SAMP, T_IDX, nT))
                        r, w = 2 * NS, PAST + NS
                        rows = slice(NS * jb[1], NS * (jb[1] + 1))
                        l = logit(SAMP, w, r)
                        v.tensor_tensor(l[rows, 0:PAST], ps[rows, bank, 0:PAST], C("pastbias", r)[rows], ALU.add)
                        m = v.tensor_tensor(l[rows, PAST:w], ps[rows, bank, PAST:w],
                                            C("newbias", r)[rows, bass.ds(i * NS, NS)], ALU.add)
                    m.then_inc(s_su, 1)
                    if jb == ("samp", 0):
                        return
                    dve.wait_ge(s_su, nS * i + k + 3)
                    s_ = slot(jb)
                    v.tensor_reduce(nmax[0:r, s_:s_ + 1], l, AX, ALU.max, negate=True).then_inc(s_max, 1)

                def invert(jb, r):
                    dve.wait_ge(s_exp, nT * i + T_IDX[jb] + 1)
                    sl_ = ssum[0:r, slot(jb):slot(jb) + 1]
                    v.reciprocal(sl_, sl_).then_inc(s_inv, 1)
                    dve.wait_ge(s_inv, nT * i + INV_IDX[jb] + 1)

                def normalise():
                    invert(SAMP, 2 * NS)
                    l = logit(SAMP, PAST + NS, 2 * NS)
                    v.tensor_scalar(l, l, ssum[0:2 * NS, 4:5], None, ALU.mult).then_inc(s_pn, 1)

                def products(jb):
                    k = O_IDX[jb]
                    bank = o_bank(jb)
                    if jb[0] == "reto":
                        dve.wait_ge(s_stg, 6 * i + 5)
                    if jb[0] == "rets":
                        dve.wait_ge(s_rst, 16 * i + 16)
                    if jb[0] == "moba":
                        invert(jb, P)
                    dve.wait_ge(s_o, nO * i + nO + k + 1)
                    if jb[0] == "moba":
                        _, u, qb = jb
                        m = v.tensor_scalar(om[:, qb, bass.ds((2 * i + u) * DH, DH)], ps[:, bank, 0:DH],
                                            ssum[:, qb:qb + 1], None, ALU.mult)
                    elif jb[0] == "samp":
                        b = 2 * i + jb[1]
                        o = ps[:, bank, 0:32].rearrange("p (c h q) -> p c h q", c=4, h=2)
                        for h in range(2):
                            m = v.tensor_copy(oTs[DH * h:DH * (h + 1), 4:8, bass.ds(SL * b, SL)],
                                              o[DH * h:DH * (h + 1), :, h, :])
                    elif jb[0] == "skv":
                        for h in range(RH):
                            st = st_b[:, jb[1], h, :]
                            m = v.scalar_tensor_tensor(st, st, float(GAMMAS[h] ** SL), ps[:, bank, h * P:(h + 1) * P],
                                                       ALU.mult, ALU.add)
                    elif jb[0] == "reto":
                        v.tensor_copy(rk_t[:, 0:4, bass.ds(i * P, P)], ps[:, bank, :].rearrange("p (t n) -> p t n", t=4))
                        for qb in range(4):
                            m = v.bn_stats(gstat[:, bass.ds(i * TT + qb, 1), :].rearrange("p o c -> p (o c)"),
                                           ps[:, bank, qb * P:(qb + 1) * P])
                    else:
                        m = v.tensor_copy(rst, ps[:, bank, 0:P])
                    m.then_inc(s_ou, 1)

                for kind, jb in ORDER:
                    if kind == "S":
                        scores(jb)
                    elif kind == "N":
                        normalise()
                    elif kind == "O":
                        products(jb)

            dve.wait_ge(s_cross, 1 + SB)
            v.tensor_copy(rk_t[0:NS, 4, :], ps[0:NS, XBANK, :])
            for h in range(RH):
                m = v.bn_stats(gstat[0:NS, h * TT + 4, :], ps[0:NS, XBANK, h * P:(h + 1) * P])
            ch.link(m)
            for h in range(RH):
                for t in range(TT):
                    r = P if t < 4 else NS
                    m = v.bn_aggr(gmv[0:r, h * TT + t, :], gstat[0:r, h * TT + t, :])
            m.then_inc(s_gst, 1)
            dve.wait_ge(s_gsq, 1)
            gs = gstd[:].rearrange("p (h t) -> p h t", h=RH)
            v.reciprocal(gs[:, :, 0:4], gs[:, :, 0:4])
            ch.link(v.reciprocal(gs[0:NS, :, 4], gs[0:NS, :, 4]))
            for t in range(TT):
                r = P if t < 4 else NS
                for h in range(RH):
                    o = rk_t[0:r, t, h * P:(h + 1) * P]
                    n = h * TT + t
                    m = v.tensor_scalar(o, o, gmv[0:r, n, 0:1], gstd[0:r, n:n + 1], ALU.subtract, ALU.mult)
                ch.link(m)
                v.tensor_tensor(rg_t[0:r, t, :], rg_t[0:r, t, :], rk_t[0:r, t, :], ALU.mult).then_inc(s_gn, 1)

            split_weights(0, 1, 16 * 12, 28, s_bsp)
            dve.wait_ge(s_xcl, 1)
            for t in range(TT):
                r = P if t < 4 else NS
                b = 4 + 2 * (t % 2)
                for q in range(2):
                    dve.wait_ge(s_otc, 2 * t + q + 1)
                    o = (slice(None), slice(4 * q, 4 * q + 4), slice(t * P, t * P + r))
                    if q == 1 and t == 4:
                        src = oTs[:, 4:8, :]
                    else:
                        src = ps[:, b + q, :].rearrange("p (c n) -> p c n", c=4)[:, :, 0:r]
                    v.tensor_tensor(o_lo[o], src, o_hi[o].bitcast(F32), ALU.subtract).then_inc(s_olo, 1)

            def merge(n, u):
                dve.wait_ge(s_cgs, n + 3)
                dve.wait_ge(s_cb, n + 1)
                at = bass.ds(n, 1) if not isinstance(n, int) else slice(n, n + 1)
                mg = merged[:, at, :].rearrange("p o (h c) -> p (o h) c", h=2)
                tb = t_b[:, u].rearrange("p (h c) -> p h c", h=2)
                v.tensor_tensor(mg, mg, ps[:, 4:6, 0:HALF], ALU.mult)
                v.tensor_tensor(tb, gb_s[:, u].rearrange("p (h c) -> p h c", h=2), ps[:, 6:8, 0:HALF], ALU.mult
                                ).then_inc(s_cbu, 1)
                dve.wait_ge(s_cbu, n + 2)
                v.tensor_tensor(mg, mg, tb, ALU.add).then_inc(s_mg, 1)

            dve.wait_ge(s_gas, 1)
            with dve.Fori(0, 3) as i:
                for u in range(2):
                    n = 2 * i + u
                    dve.wait_ge(s_cg, n + 2)
                    split_weights(1, 2 * u, 16 * ([12, 8][u] + 1 + i), 29 + 2 * n, s_gsp)
                    dve.wait_ge(s_cb, n + 1)
                    split_weights(0, 2 * (1 - u) + 1, 16 * ([8, 12][u] + i + u), 30 + 2 * n, s_bsp)
                    merge(n, u)
            dve.wait_ge(s_cb, 7)
            split_weights(0, 3, 16 * 11, 41, s_bsp)
            for n in (6, 7):
                merge(n, n % 2)

            def row_stats(n, z, r):
                for q in range(2):
                    m = v.bn_stats(lst[0:r, n % 2, q, :], z[:, q * 512:(q + 1) * 512])
                ch.link(m)
                v.bn_aggr(lmv[0:r, n % 2], lst[0:r, n % 2].rearrange("p a b -> p (a b)")).then_inc(s_var, 1)

            def inverse_std(n, r):
                dve.wait_ge(s_std, n + 1)
                ch.link(v.reciprocal(lsd[0:r, n:n + 1], lsd[0:r, n:n + 1]))

            dve.wait_ge(s_x, 32)
            dve.wait_ge(s_ln1, 32)
            for t in range(TT):
                r = P if t < 4 else NS
                z = x_tm[0:r, t, :]
                dve.wait_ge(s_y, t + 1)
                for q in range(2):
                    m = v.scalar_tensor_tensor(z[:, q * 512:(q + 1) * 512], z[:, q * 512:(q + 1) * 512], ALPHA,
                                               ps[0:r, 2 * (t % 2) + q, :], ALU.mult, ALU.add)
                m.then_inc(s_yu, 1)
                dve.wait_ge(s_yu, t + 1)
                row_stats(t, z, r)
                dve.wait_ge(s_var, t + 1)
                ch.link(v.scalar_tensor_tensor(z, z, lmv[0:r, t % 2, 0:1], ln_g[0:r], ALU.subtract, ALU.mult))
                inverse_std(t, r)
                v.scalar_tensor_tensor(z, z, lsd[0:r, t:t + 1], ln_b[0:r], ALU.mult, ALU.add).then_inc(s_x1, 1)

            L = ch.link
            tt_, ts_, tr_ = v.tensor_tensor, v.tensor_scalar, v.tensor_reduce

            def tmp(o, *shape):
                n = int(np.prod(shape))
                a = rtr[:, o:o + n]
                if len(shape) == 2:
                    a = a.rearrange("p (a b) -> p a b", a=shape[0])
                elif len(shape) == 3:
                    a = a.rearrange("p (a b c) -> p a b c", a=shape[0], b=shape[1])
                return a

            sel = tmp(0, TT, NE)
            s1, s2 = tmp(160, TT, NG, EPG), tmp(320, TT, NG, EPG)
            es4 = tmp(480, TT, NG, EPG)
            pos, ge = tmp(640, TT, NE), tmp(800, TT, NE)
            e5 = [tmp(960 + 40 * k, TT, EPG) for k in range(5)]
            g5 = [tmp(1160 + 20 * k, TT, NG) for k in range(4)]
            f5 = [tmp(1300 + 5 * k, TT) for k in range(12)]
            c32 = [tmp(1400 + 32 * k, NE) for k in range(5)]
            ev = tmp(1600, OVT, NE)
            evs = tmp(2260, 64)
            L(v.memset(logs, 0.0))
            dve.wait_ge(s_lg, TT)
            dve.wait_ge(s_par, 64)
            lp = ps[:, 6, 0:TT * 36].rearrange("p (t n) -> p t n", t=TT)
            tt_(logs[:, 0:4], lp[:, 0:4], br[:].unsqueeze(1).to_broadcast([P, 4, 36]), ALU.add)
            L(tt_(logs[0:NS, 4], lp[0:NS, 4], br[0:NS], ALU.add))

            def bc(a, n):
                return a.unsqueeze(2).to_broadcast([P, TT, n])

            def first_max(src, ramp, n, peak, eq, low, onehot):
                L(tr_(peak, src, AX, ALU.max))
                L(tt_(eq, src, bc(peak, n), ALU.is_ge))
                L(v.scalar_tensor_tensor(eq, eq, -64.0, C(ramp).unsqueeze(1).to_broadcast([P, TT, n]),
                                         ALU.mult, ALU.add))
                L(tr_(low, eq, AX, ALU.min))
                L(tt_(onehot, eq, bc(low, n), ALU.is_equal))

            gl = logs[:, :, 0:NG]
            el = logs[:, :, NG:NG + NE].rearrange("p t (g e) -> p t g e", g=NG)
            gmax, m1, m2, low, gsum, w1, slf = f5[0:7]
            first_max(gl, "i4", NG, gmax, g5[0], low, g5[1])
            tt_(dgl, gl, bc(gmax, NG), ALU.subtract).then_inc(s_gexp_i, 1)
            L(tt_(g5[2], g5[1], bc(C("valid"), NG), ALU.mult))
            L(tt_(es4, el, g5[1].unsqueeze(3).to_broadcast([P, TT, NG, EPG]), ALU.mult))
            es, es2, oh1, oh2, eq8 = e5
            L(tr_(es, es4.rearrange("p t g e -> p t e g"), AX, ALU.add))
            first_max(es, "i8", EPG, m1, eq8, low, oh1)
            L(v.scalar_tensor_tensor(es2, oh1, -BIG, es, ALU.mult, ALU.add))
            first_max(es2, "i8", EPG, m2, eq8, low, oh2)
            tt_(dm, m2, m1, ALU.subtract).then_inc(s_gexp_i, 1)
            for s_, oh in ((s1, oh1), (s2, oh2)):
                m = tt_(s_, oh.unsqueeze(2).to_broadcast([P, TT, NG, EPG]),
                        g5[2].unsqueeze(3).to_broadcast([P, TT, NG, EPG]), ALU.mult)
            L(m)
            flat = "p t g e -> p t (g e)"
            tt_(sel, s1.rearrange(flat), s2.rearrange(flat), ALU.add).then_inc(s_msk, 1)
            dve.wait_ge(s_gexp, 1)
            L(tr_(gsum, dgl, AX, ALU.add))
            dve.wait_ge(s_gexp, 2)
            L(ts_(w1, dm, 1.0, None, ALU.add))
            L(tt_(w1, w1, gsum, ALU.mult))
            L(v.reciprocal(wts[:, 0, :], w1))
            L(tt_(wts[:, 1, :], wts[:, 0, :], dm, ALU.mult))
            dve.wait_ge(s_pre, 1)
            tot, nov_, incl, off, one = c32
            rank = ps[:, 7, 0:TT * NE].rearrange("p (t e) -> p t e", t=TT)
            v.tensor_copy(tot, ps[:, 7, TT * NE:(TT + 1) * NE])
            v.memset(one, 1.0)
            L(v.tensor_copy(pos, rank))
            more = T // CAP
            over = tmp(1600, NE, more)
            L(tt_(over, tot.unsqueeze(2).to_broadcast([P, NE, more]),
                  C("e64")[:, 1:more + 1].unsqueeze(1).to_broadcast([P, NE, more]), ALU.is_gt))
            L(tr_(nov_, over, AX, ALU.add))
            L(v.tensor_tensor_scan(incl, one, nov_, 0.0, ALU.mult, ALU.add))
            L(tt_(off, incl, nov_, ALU.subtract))
            L(ts_(off, off, float(CAP), float(CAP * (NE - 1)), ALU.mult, ALU.add))
            L(tt_(off, off, C("e64"), ALU.subtract))
            b32 = [P, TT, NE]
            L(ts_(ge, pos, float(CAP), None, ALU.is_ge))
            L(tt_(ge, ge, off.unsqueeze(1).to_broadcast(b32), ALU.mult))
            L(tt_(pos, pos, C("e64").unsqueeze(1).to_broadcast(b32), ALU.add))
            L(tt_(pos, pos, ge, ALU.add))
            for c, s_ in enumerate((s1, s2)):
                L(tt_(ge, pos, s_.rearrange(flat), ALU.mult))
                L(tr_(slf, ge, AX, ALU.add))
                L(v.tensor_copy(slot_i[:, c, :], slf))
            lo_i, hi_i = lohi[:, 0], lohi[:, 1]
            L(ts_(lo_i, slot_i[:], P - 1, None, ALU.bitwise_and))
            L(ts_(hi_i, slot_i[:], 7, None, ALU.logical_shift_right))
            lof, hif = tmp(2230, 2, TT), tmp(2240, 2, TT)
            v.tensor_copy(lof, lo_i)
            L(v.tensor_copy(hif, hi_i))
            for c in range(2):
                o = slice(c * TT, (c + 1) * TT)
                v.tensor_tensor(oh_lo[:, o], C("iota").unsqueeze(1).to_broadcast([P, TT, P]),
                                lof[:, c].unsqueeze(2).to_broadcast([P, TT, P]), ALU.is_equal)
                L(v.tensor_tensor(oh_hi[:, o], C("iota")[:, 0:COLS].unsqueeze(1).to_broadcast([P, TT, COLS]),
                                  hif[:, c].unsqueeze(2).to_broadcast([P, TT, COLS]), ALU.is_equal))
                v.tensor_tensor(oh_hi[:, o], oh_hi[:, o], C("tokid").unsqueeze(2).to_broadcast([P, TT, COLS]),
                                ALU.mult).then_inc(s_oh, 1)
            dve.wait_ge(s_ohu, 1)
            v.tensor_copy(idx_i[:], ps[:, 6, 256:256 + COLS]).then_inc(s_idx, 1)
            i1 = incl[0:1]
            L(tt_(ev[0:1], i1.unsqueeze(1).to_broadcast([1, OVT, NE]),
                  C("iv", 1).unsqueeze(2).to_broadcast([1, OVT, NE]), ALU.is_le))
            L(tr_(evs[0:1, 0:OVT], ev[0:1], AX, ALU.add))
            L(v.memset(ev_i[:], 0))
            L(ts_(ev_i[0:1, 0:OVT], evs[0:1, 0:OVT], float(NE - 1), None, ALU.min))
            L(ts_(evs[0:1, 32:32 + OVP], C("iota", 1)[:, 0:OVP], 2.0, incl[0:1, NE - 1:NE], ALU.mult, ALU.is_lt))
            L(tr_(evs[0:1, 50:51], evs[0:1, 32:32 + OVP], AX, ALU.add))
            v.tensor_copy(ev_i[0:1, 2 * OVP:2 * OVP + 1], evs[0:1, 50:51]).then_inc(s_nov, 1)

            def hidden(n, u):
                dve.wait_ge(s_sl, n + 1)
                v.tensor_tensor(hid[:, u], sg[:, u], ps[:, 2 + u, P:2 * P], ALU.mult).then_inc(s_h, 1)

            def expert_rows(n, u, free):
                dve.wait_ge(s_dn, n + 1)
                free()
                for q in range(2):
                    m = v.tensor_copy(yo[:, u, q * 512:(q + 1) * 512], ps[:, 4 + 2 * u + q, :])
                m.then_inc(s_ye, 1)

            def four_pairs(i):
                for q in range(4):
                    n, u = 4 * i + q, q % 2
                    hidden(n, u)
                    if not (isinstance(n, int) and n == 0):
                        expert_rows(n - 1, 1 - u, lambda: dve.wait_ge(s_ys[1 - u], 16 * (2 * i + (q - 1) // 2 + 1)))

            four_pairs(0)
            with dve.Fori(1, 4) as i:
                four_pairs(i)
            expert_rows(PAIRS - 1, 1, lambda: dve.wait_ge(s_ys[1], 16 * (PAIRS // 2)))
            dve.wait_ge(s_nov, 1)
            nov = dve.value_load(ev_i[0:1, 2 * OVP:2 * OVP + 1], min_val=0, max_val=OVP)
            with dve.If(nov > 0):
                with dve.Fori(0, nov) as i:
                    v.tensor_copy(idx_o[:], idx_i[:, bass.ds(PAIRS + i, 1)]).then_inc(s_ovi, 1)
                    hidden(PAIRS + i, 0)

                    def free():
                        dve.wait_ge(s_ys[0], 16 * PAIRS // 2 + 16)
                        dve.wait_ge(s_ovs, 16 * i + 16)
                    expert_rows(PAIRS + i, 0, free)

            def weigh(t):
                r = P if t < 4 else NS
                z = x_tm[0:r, t, :]
                dve.wait_ge(s_xa, t + 1)
                dve.wait_ge(s_yg[t % 4], 32 * (t // 4 + 1))
                for c in range(2):
                    m = v.scalar_tensor_tensor(z, picked[0:r, t % 4, c], wts[0:r, c, t:t + 1], z, ALU.mult, ALU.add)
                    if c == 0:
                        L(m)
                m.then_inc(s_fru, 1)
                dve.wait_ge(s_fru, t + 1)
                row_stats(TT + t, z, r)

            def shift(t):
                r, n = (P if t < 4 else NS), TT + t
                inverse_std(n, r)
                v.scalar_tensor_tensor(lsh[0:r, n:n + 1], lmv[0:r, n % 2, 0:1], -1.0,
                                       lsd[0:r, n:n + 1], ALU.mult, ALU.mult).then_inc(s_shift, 1)

            def gain(t):
                r = P if t < 4 else NS
                dve.wait_ge(s_nrm, t + 1)
                v.tensor_tensor(x_tm[0:r, t, :], x_tm[0:r, t, :], ln_g[0:r], ALU.mult).then_inc(s_gain, 1)

            dve.wait_ge(s_ln2, 32)
            for t in range(TT):
                weigh(t)
                if t > 0:
                    shift(t - 1)
                if t > 1:
                    gain(t - 2)
            shift(TT - 1)
            gain(TT - 2)
            gain(TT - 1)
            dve.wait_ge(s_gain, TT)
            z = x_tm[0:NS, TT - 1, :]
            v.tensor_tensor(z, z, ln_b[0:NS], ALU.add).then_inc(s_finl, 1)


def kernel(x_prompt, x_sample, cache_k, cache_v, state_ret, page_table, w_in, b_merge, gn_g, w_br_ret, w_br_moba,
           w_out, ln1_g, ln1_b, w_router_group, b_router_group, w_router_expert, b_router_expert, w_exp_gate,
           w_exp_up, w_exp_down, ln2_g, ln2_b):
    import concourse.bacc as bacc
    from concourse.bass_utils import run_bass_kernel_spmd

    def c(a):
        return np.ascontiguousarray(a)

    def tiles(w):
        k, n = w.shape
        return w.reshape(k // P, P, n // P, P).transpose(2, 1, 0, 3).reshape(n // P, P, k)

    x = np.concatenate([np.asarray(x_prompt).reshape(NP, D), np.asarray(x_sample).reshape(NS, D)], 0)
    w = np.asarray(w_in)[0]
    at = dict(zip((RQ, RK, RV, RG, MQ, MK, MV), range(0, 7 * G, G)))
    order = [w[:, at[g]:at[g] + G] for g in (MK, RK, RV, RG, MV, MQ, RQ)] + [w[:, 7 * G:7 * G + D]]
    first = tiles(np.concatenate(order, 1))
    second = tiles(w[:, 7 * G + D:])
    branch = np.concatenate([tiles(np.asarray(w_br_ret)[0]), tiles(np.asarray(w_br_moba)[0])], 2)
    both = np.stack([second, branch], 1).reshape(2 * KD, P, D)
    gate_up = np.concatenate([np.asarray(w_exp_gate)[0], np.asarray(w_exp_up)[0]], 2).reshape(NE, KD, P, 2 * P)
    ck = np.asarray(cache_k)[0]
    n_pool = ck.shape[0]
    wrt = np.concatenate([np.asarray(w_router_group)[0],
                          np.asarray(w_router_expert)[0].transpose(1, 0, 2).reshape(D, NE)], 1)
    arrays = {
        "xT": c(x.T.reshape(KD, P, T).transpose(1, 0, 2)),
        "x": c(x),
        "w_tiles": c(np.concatenate([first, both], 0)),
        "w_out": c(np.asarray(w_out)[0]),
        "w_router": c(wrt.reshape(KD, P, NG + NE).transpose(1, 0, 2)),
        "b_router": c(np.concatenate([np.asarray(b_router_group)[0], np.asarray(b_router_expert)[0].reshape(NE)])),
        "b_merge": c(np.asarray(b_merge)[0].reshape(2 * KD, P).T),
        "gn_g": c(np.asarray(gn_g)[0]),
        "ln1_g": c(np.asarray(ln1_g)[0]), "ln1_b": c(np.asarray(ln1_b)[0]),
        "ln2_g": c(np.asarray(ln2_g)[0]), "ln2_b": c(np.asarray(ln2_b)[0]),
        "experts": c(np.concatenate([gate_up.transpose(0, 2, 1, 3).reshape(NE, P, 2 * D), np.asarray(w_exp_down)[0]], 2)),
        "kT_pool": c(ck.reshape(n_pool, PAGE, 4, P).transpose(0, 2, 3, 1)),
        "v_pool": c(np.asarray(cache_v)[0].reshape(n_pool, PAGE, G)),
        "page_table": c(np.asarray(page_table).reshape(1, SB * NPG)),
        "state": c(np.asarray(state_ret)),
        "constants": constants(),
    }
    outs = [(1, NP, D), (SB, SL, D), (1, 1, NP, MH, DH), (1, 1, NP, MH, DH), (1, 1, RH, P, P),
            (1, SB, SL, MH, DH), (1, SB, SL, MH, DH), (1, SB, RH, P, P)]
    nc = bacc.Bacc("TRN2", target_bir_lowering=False, num_devices=1)
    args = [nc.dram_tensor(n, a.shape, mybir.dt.from_np(a.dtype), kind="ExternalInput").ap()
            for n, a in arrays.items()]
    args += [nc.dram_tensor(f"out_{n}", s, F32, kind="ExternalOutput").ap() for n, s in enumerate(outs)]
    args.append(nc.dram_tensor("x1_rows", (T, D), F32, kind="Internal").ap())
    args.append(nc.dram_tensor("slot_rows", (COLS * P, D), F32, kind="Internal").ap())
    hybrid_step(nc, *args)
    r = run_bass_kernel_spmd(nc, [arrays], core_ids=[0])
    return tuple(r.results[0][f"out_{n}"] for n in range(len(outs)))
```
